# Optimizing a Trainium2 kernel written in Bass

```python
import jax, jax.numpy as jnp
from jax import lax
import numpy as np

D_MODEL = 2048
BATCH = 1
SEQ = 256
DEPTH = 1

HEAD_DIM = 64
A_HEADS = 8
A_WIDTH = A_HEADS * HEAD_DIM
CHUNK = 128
B_WIDTH = 768
CONV_WIDTH = 3
DILATION_PATTERNS = ((128, 1), (512, 4), (2048, 16))
C_HEADS_PER_PATTERN = 4
C_HEADS = C_HEADS_PER_PATTERN * len(DILATION_PATTERNS)
C_WIDTH = C_HEADS * HEAD_DIM
D_MIX = A_WIDTH + B_WIDTH + C_WIDTH
PROJ_SIZES = (A_WIDTH, A_WIDTH, B_WIDTH, B_WIDTH, B_WIDTH, C_WIDTH, C_WIDTH, C_WIDTH)
PROJ_SPLITS = tuple(int(s) for s in np.cumsum(PROJ_SIZES)[:-1])
D_IN_PROJ = sum(PROJ_SIZES)
D_FF = 4 * D_MODEL
EPS = 1e-6


def rms_norm(x, g):
    x32 = x.astype(jnp.float32)
    y = x32 * lax.rsqrt(jnp.mean(x32 * x32, axis=-1, keepdims=True) + EPS)
    return (y * g.astype(jnp.float32)).astype(x.dtype)

def spatial_gating(u, v, w_s, b_s):
    bsz, s = u.shape[:2]
    n_chunks = s // CHUNK
    vc = v.reshape(bsz, n_chunks, CHUNK, A_HEADS, HEAD_DIM)
    w_causal = jnp.tril(w_s)
    mixed = jnp.einsum('hij,bcjhd->bcihd', w_causal, vc) + b_s.T[None, None, :, :, None]
    return u * mixed.reshape(bsz, s, A_WIDTH)

def short_gated_conv(b_gate, c_gate, xb, w_conv):
    z = c_gate * xb
    zp = jnp.pad(z, ((0, 0), (CONV_WIDTH - 1, 0), (0, 0)))
    s = z.shape[1]
    conv = sum(w_conv[i] * zp[:, i:i + s] for i in range(CONV_WIDTH))
    return b_gate * conv

def head_rms_norm(x, g):
    x32 = x.astype(jnp.float32)
    return x32 * lax.rsqrt(jnp.mean(x32 * x32, axis=-1, keepdims=True) + EPS) * g.astype(jnp.float32)

def dilated_window_attention(q, k, v, window, dilation):
    bsz, s, h, d = q.shape
    length = s // dilation
    blk = window // dilation
    nb = -(-length // blk)
    lp = nb * blk

    def to_sub(t):
        t = t.reshape(bsz, length, dilation, h, d).transpose(0, 2, 1, 3, 4)
        t = jnp.pad(t, ((0, 0), (0, 0), (0, lp - length), (0, 0), (0, 0)))
        return t.reshape(bsz, dilation, nb, blk, h, d)

    qb = to_sub(q)
    kb = to_sub(k)
    vb = to_sub(v.astype(jnp.float32))
    pad_prev = ((0, 0), (0, 0), (1, 0), (0, 0), (0, 0), (0, 0))
    kcat = jnp.concatenate([jnp.pad(kb, pad_prev)[:, :, :-1], kb], axis=3)
    vcat = jnp.concatenate([jnp.pad(vb, pad_prev)[:, :, :-1], vb], axis=3)

    scores = jnp.einsum('brnqhd,brnkhd->brnhqk', qb, kcat) * (HEAD_DIM ** -0.5)
    qi = jnp.arange(blk)[:, None]
    kj = jnp.arange(2 * blk)[None, :]
    band = (kj >= qi) & (kj <= qi + blk)
    has_prev = jnp.arange(nb)[:, None, None] > 0
    mask = band[None] & (has_prev | (kj >= blk)[None])
    scores = jnp.where(mask[None, None, :, None], scores, -jnp.inf)
    m = jnp.max(scores, axis=-1, keepdims=True)
    e = jnp.exp(scores - m)
    den = jnp.sum(e, axis=-1, keepdims=True)
    o = jnp.einsum('brnhqk,brnkhd->brnhqd', e, vcat) / den
    lse = (m + jnp.log(den))[..., 0]

    o = o.transpose(0, 1, 2, 4, 3, 5).reshape(bsz, dilation, lp, h, d)[:, :, :length]
    o = o.transpose(0, 2, 1, 3, 4).reshape(bsz, s, h, d)
    lse = lse.transpose(0, 1, 2, 4, 3).reshape(bsz, dilation, lp, h)[:, :, :length]
    lse = lse.transpose(0, 2, 1, 3).reshape(bsz, s, h)
    return o, lse

def dilated_mixture(q, k, v, q_g, k_g):
    bsz, s = q.shape[:2]
    q = head_rms_norm(q.reshape(bsz, s, C_HEADS, HEAD_DIM), q_g)
    k = head_rms_norm(k.reshape(bsz, s, C_HEADS, HEAD_DIM), k_g)
    v = v.reshape(bsz, s, C_HEADS, HEAD_DIM)
    outs, lses = [], []
    for g, (window, dilation) in enumerate(DILATION_PATTERNS):
        sl = slice(g * C_HEADS_PER_PATTERN, (g + 1) * C_HEADS_PER_PATTERN)
        o, lse = dilated_window_attention(q[:, :, sl], k[:, :, sl], v[:, :, sl], window, dilation)
        outs.append(o)
        lses.append(lse)
    alpha = jax.nn.softmax(jnp.stack(lses, axis=0), axis=0)
    y = jnp.stack(outs, axis=0) * alpha[..., None]
    return y.transpose(1, 2, 0, 3, 4).reshape(bsz, s, C_WIDTH).astype(v.dtype)

def first_inputs(seed: int = 0) -> dict:
    key = jax.random.key(seed)
    ks = jax.random.split(key, 12)
    n = jax.random.normal
    f32 = jnp.float32
    return {
        'x': n(ks[0], (BATCH, SEQ, D_MODEL), f32),
        'attn_norm': 1.0 + 0.02 * n(ks[1], (DEPTH, D_MODEL), f32),
        'w_in': n(ks[2], (DEPTH, D_MODEL, D_IN_PROJ), f32) * D_MODEL ** -0.5,
        'sgu_w': n(ks[3], (DEPTH, A_HEADS, CHUNK, CHUNK), f32) * CHUNK ** -0.5,
        'sgu_b': 1.0 + 0.1 * n(ks[4], (DEPTH, A_HEADS, CHUNK), f32),
        'conv_w': n(ks[5], (DEPTH, CONV_WIDTH, B_WIDTH), f32) * CONV_WIDTH ** -0.5,
        'q_norm': 1.0 + 0.02 * n(ks[6], (DEPTH, HEAD_DIM), f32),
        'k_norm': 1.0 + 0.02 * n(ks[7], (DEPTH, HEAD_DIM), f32),
        'w_out': n(ks[8], (DEPTH, D_MIX, D_MODEL), f32) * D_MIX ** -0.5,
        'mlp_norm': 1.0 + 0.02 * n(ks[9], (DEPTH, D_MODEL), f32),
        'w_mlp_in': n(ks[10], (DEPTH, D_MODEL, D_FF), f32) * D_MODEL ** -0.5,
        'w_mlp_out': n(ks[11], (DEPTH, D_FF, D_MODEL), f32) * D_FF ** -0.5,
    }

def first_block(x, attn_norm, w_in, sgu_w, sgu_b, conv_w, q_norm, k_norm, w_out,
              mlp_norm, w_mlp_in, w_mlp_out):
    for l in range(DEPTH):
        h = rms_norm(x, attn_norm[l])
        p = h @ w_in[l]
        a_u, a_v, b_b, b_c, b_x, q, k, v = jnp.split(p, PROJ_SPLITS, axis=-1)
        y_a = spatial_gating(a_u, a_v, sgu_w[l], sgu_b[l])
        y_b = short_gated_conv(b_b, b_c, b_x, conv_w[l])
        y_c = dilated_mixture(q, k, v, q_norm[l], k_norm[l])
        x = x + jnp.concatenate([y_a, y_b, y_c], axis=-1) @ w_out[l]
        h = rms_norm(x, mlp_norm[l])
        x = x + jnp.square(jax.nn.relu(h @ w_mlp_in[l])) @ w_mlp_out[l]
    return x


GRID_W = 64
MIX_W = D_MODEL
RWKV_W = MIX_W // 2
ATTN_W = MIX_W - RWKV_W
RWKV_HEADS = RWKV_W // HEAD_DIM
ATTN_Q_HEADS = ATTN_W // HEAD_DIM
ATTN_KV_HEADS = 4
KV_GROUPS = ATTN_Q_HEADS // ATTN_KV_HEADS
KV_W = ATTN_KV_HEADS * HEAD_DIM
DECAY_LORA = 96
AAA_LORA = 96
GATE_LORA = 256
GN_EPS = 64e-5
ROPE_THETA = 10000.0
ROPE_AXIS_DIM = HEAD_DIM // 2
Q_BLOCK = 128
NORM_EPS = 1e-6
PEER_HEADS = 8
PEER_KEY_DIM = 256
PEER_HALF = PEER_KEY_DIM // 2
N_KEYS = 128
N_EXPERTS = N_KEYS * N_KEYS
PEER_TOPK = 16
PEER_CHUNK = 128

RWKV_SPLITS = (RWKV_W, 2 * RWKV_W, 3 * RWKV_W,
               3 * RWKV_W + DECAY_LORA, 3 * RWKV_W + 2 * DECAY_LORA,
               3 * RWKV_W + 2 * DECAY_LORA + AAA_LORA, 3 * RWKV_W + 2 * DECAY_LORA + 2 * AAA_LORA)
RWKV_COLS = 3 * RWKV_W + 2 * DECAY_LORA + 2 * AAA_LORA + GATE_LORA
IN_SPLITS = (RWKV_COLS, RWKV_COLS + ATTN_W, RWKV_COLS + ATTN_W + KV_W)
IN_COLS = RWKV_COLS + ATTN_W + 2 * KV_W


def rmsnorm(x, w):
    xf = x.astype(jnp.float32)
    y = xf * lax.rsqrt(jnp.mean(xf * xf, axis=-1, keepdims=True) + NORM_EPS)
    return (y * w.astype(jnp.float32)).astype(x.dtype)

def centred_shift(z, mu_prev, mu_next):
    zp = jnp.pad(z[:, :-1], ((0, 0), (1, 0), (0, 0)))
    zn = jnp.pad(z[:, 1:], ((0, 0), (0, 1), (0, 0)))
    return z + mu_prev * (zp - z) + mu_next * (zn - z)

def rwkv7_bidir(z, mu_prev, mu_next, w0, w2, a0, a2, g2, k_k, k_a, r_k, lnx_w, lnx_b):
    B, S, _ = z.shape
    H, N = RWKV_HEADS, HEAD_DIM
    f32 = jnp.float32
    z = centred_shift(z.astype(f32), mu_prev.astype(f32), mu_next.astype(f32))
    r, k, v, wl_f, wl_b, al_f, al_b, gl = jnp.split(z, RWKV_SPLITS, axis=-1)
    wl = jnp.stack([wl_f, wl_b])
    al = jnp.stack([al_f, al_b])
    w_log = -jax.nn.softplus(-(w0.astype(f32)[:, None, None, :]
                               + jnp.einsum('nbsl,nlc->nbsc', jnp.tanh(wl), w2.astype(f32)))) - 0.5
    decay = jnp.exp(-jnp.exp(w_log))
    a = jax.nn.sigmoid(a0.astype(f32)[:, None, None, :]
                       + jnp.einsum('nbsl,nlc->nbsc', al, a2.astype(f32)))
    g = jax.nn.sigmoid(gl) @ g2.astype(f32)
    kk = (k * k_k.astype(f32)).reshape(B, S, H, N)
    kk = kk / jnp.maximum(jnp.sqrt(jnp.sum(kk * kk, axis=-1, keepdims=True)), 1e-12)
    kk = kk.reshape(B, S, RWKV_W)
    k_dir = k[None] * (1.0 + (a - 1.0) * k_a.astype(f32))
    ka = kk[None] * a

    def dir_seq(arr):
        arr = jnp.stack([arr[0], arr[1][:, ::-1]])
        return jnp.moveaxis(arr.reshape(2, B, S, H, N), 2, 0)

    xs = (dir_seq(jnp.stack([r, r])), dir_seq(decay), dir_seq(k_dir),
          dir_seq(jnp.stack([v, v])), dir_seq(jnp.stack([kk, kk])), dir_seq(ka))

    def step(state, inp):
        r_t, w_t, k_t, v_t, kk_t, ka_t = inp
        sa = jnp.einsum('dbhij,dbhj->dbhi', state, -kk_t)
        state = (state * w_t[..., None, :] + sa[..., :, None] * ka_t[..., None, :]
                 + v_t[..., :, None] * k_t[..., None, :])
        y = jnp.einsum('dbhij,dbhj->dbhi', state, r_t)
        return state, y

    state0 = jnp.zeros((2, B, H, N, N), f32)
    _, ys = lax.scan(step, state0, xs)
    ys = jnp.moveaxis(ys, 0, 2)
    y = ys[0] + ys[1][:, ::-1]
    mu = jnp.mean(y, axis=-1, keepdims=True)
    var = jnp.mean(jnp.square(y - mu), axis=-1, keepdims=True)
    y = ((y - mu) * lax.rsqrt(var + GN_EPS)).reshape(B, S, RWKV_W)
    y = y * lnx_w.astype(f32) + lnx_b.astype(f32)
    k_mean = jnp.mean(k_dir, axis=0).reshape(B, S, H, N)
    bonus = jnp.sum(r.reshape(B, S, H, N) * k_mean * r_k.astype(f32), axis=-1, keepdims=True) \
        * v.reshape(B, S, H, N)
    return (y + bonus.reshape(B, S, RWKV_W)) * g

def axial_rope_tables(S):
    rows_count = S // GRID_W
    rows = jnp.repeat(jnp.arange(rows_count), GRID_W).astype(jnp.float32)
    cols = jnp.tile(jnp.arange(GRID_W), rows_count).astype(jnp.float32)
    inv = ROPE_THETA ** (-jnp.arange(0, ROPE_AXIS_DIM, 2, dtype=jnp.float32) / ROPE_AXIS_DIM)
    ang_r = rows[:, None] * inv[None]
    ang_c = cols[:, None] * inv[None]
    return jnp.cos(ang_r), jnp.sin(ang_r), jnp.cos(ang_c), jnp.sin(ang_c)

def rope_rotate(x, cos, sin):
    x1, x2 = jnp.split(x, 2, axis=-1)
    c, s = cos[None, :, None, :], sin[None, :, None, :]
    return jnp.concatenate([x1 * c - x2 * s, x2 * c + x1 * s], axis=-1)

def axial_rope(x, tabs):
    cr, sr, cc, sc = tabs
    xr, xc = x[..., :ROPE_AXIS_DIM], x[..., ROPE_AXIS_DIM:]
    return jnp.concatenate([rope_rotate(xr, cr, sr), rope_rotate(xc, cc, sc)], axis=-1)

def axial_gqa(q, k, v, q_norm_w, k_norm_w):
    B, S, _ = q.shape
    dt = q.dtype
    q = q.reshape(B, S, ATTN_Q_HEADS, HEAD_DIM)
    k = k.reshape(B, S, ATTN_KV_HEADS, HEAD_DIM)
    v = v.reshape(B, S, ATTN_KV_HEADS, HEAD_DIM)
    tabs = axial_rope_tables(S)
    q = axial_rope(rmsnorm(q, q_norm_w).astype(jnp.float32), tabs) * (HEAD_DIM ** -0.5)
    k = axial_rope(rmsnorm(k, k_norm_w).astype(jnp.float32), tabs)
    q = q.astype(dt).reshape(B, S // Q_BLOCK, Q_BLOCK, ATTN_KV_HEADS, KV_GROUPS, HEAD_DIM)
    q = jnp.moveaxis(q, 1, 0)
    k = k.astype(dt)

    def block(q_blk):
        s = jnp.einsum('bqkgd,bskd->bkgqs', q_blk, k).astype(jnp.float32)
        p = jax.nn.softmax(s, axis=-1)
        return jnp.einsum('bkgqs,bskd->bqkgd', p.astype(v.dtype), v)

    o = lax.map(block, q)
    return jnp.moveaxis(o, 0, 1).reshape(B, S, ATTN_W)

def peer_ffn(h, w_pq, sub_keys, u_tab, v_tab):
    B, S, Dm = h.shape
    T = B * S
    hf = h.reshape(T, Dm)
    q = (hf @ w_pq).reshape(T, PEER_HEADS, 2, PEER_HALF)
    s = jnp.einsum('thpc,hpnc->thpn', q, sub_keys).astype(jnp.float32)
    s1, i1 = lax.top_k(s[:, :, 0], PEER_TOPK)
    s2, i2 = lax.top_k(s[:, :, 1], PEER_TOPK)
    cand = (s1[..., :, None] + s2[..., None, :]).reshape(T, PEER_HEADS, PEER_TOPK * PEER_TOPK)
    best, ci = lax.top_k(cand, PEER_TOPK)
    e1 = jnp.take_along_axis(i1, ci // PEER_TOPK, axis=-1)
    e2 = jnp.take_along_axis(i2, ci % PEER_TOPK, axis=-1)
    expert = (e1 * N_KEYS + e2).reshape(T, PEER_HEADS * PEER_TOPK)
    gate = jax.nn.softmax(best, axis=-1).reshape(T, PEER_HEADS * PEER_TOPK).astype(h.dtype)
    nc = T // PEER_CHUNK

    def chunk(args):
        hc, ec, gc = args
        u = jnp.take(u_tab, ec, axis=0)
        act = jax.nn.gelu(jnp.einsum('cd,ckd->ck', hc, u), approximate=False) * gc
        vv = jnp.take(v_tab, ec, axis=0)
        return jnp.einsum('ck,ckd->cd', act, vv)

    out = lax.map(chunk, (hf.reshape(nc, PEER_CHUNK, Dm),
                          expert.reshape(nc, PEER_CHUNK, -1),
                          gate.reshape(nc, PEER_CHUNK, -1)))
    return out.reshape(B, S, Dm)

def second_inputs(seed: int = 0) -> dict:
    key = jax.random.key(seed)
    ks = jax.random.split(key, 32)
    L, D, C = DEPTH, D_MODEL, RWKV_W
    nrm = lambda k, shape, scale: jax.random.normal(k, shape, jnp.float32) * scale
    return {
        "x": nrm(ks[0], (BATCH, SEQ, D), 1.0),
        "w_in": nrm(ks[1], (L, D, IN_COLS), D ** -0.5),
        "mu_prev": jax.random.uniform(ks[2], (L, RWKV_COLS), jnp.float32, 0.0, 0.5),
        "mu_next": jax.random.uniform(ks[3], (L, RWKV_COLS), jnp.float32, 0.0, 0.5),
        "w0": jax.random.uniform(ks[4], (L, 2, C), jnp.float32, -6.0, -1.0),
        "w2": nrm(ks[5], (L, 2, DECAY_LORA, C), 0.5 * DECAY_LORA ** -0.5),
        "a0": nrm(ks[6], (L, 2, C), 0.1),
        "a2": nrm(ks[7], (L, 2, AAA_LORA, C), AAA_LORA ** -0.5),
        "g2": nrm(ks[8], (L, GATE_LORA, C), GATE_LORA ** -0.5),
        "k_k": 0.85 + nrm(ks[9], (L, C), 0.05),
        "k_a": 1.0 + nrm(ks[10], (L, C), 0.05),
        "r_k": nrm(ks[11], (L, RWKV_HEADS, HEAD_DIM), 0.1),
        "lnx_w": 1.0 + nrm(ks[12], (L, C), 0.02),
        "lnx_b": nrm(ks[13], (L, C), 0.01),
        "q_norm_w": 1.0 + nrm(ks[14], (L, HEAD_DIM), 0.02),
        "k_norm_w": 1.0 + nrm(ks[15], (L, HEAD_DIM), 0.02),
        "w_out": nrm(ks[16], (L, MIX_W, D), MIX_W ** -0.5),
        "norm1_w": 1.0 + nrm(ks[17], (L, D), 0.02),
        "norm2_w": 1.0 + nrm(ks[18], (L, D), 0.02),
        "w_pq": nrm(ks[19], (L, D, PEER_HEADS * PEER_KEY_DIM), D ** -0.5),
        "sub_keys": nrm(ks[20], (L, PEER_HEADS, 2, N_KEYS, PEER_HALF), PEER_HALF ** -0.5),
        "u_tab": nrm(ks[21], (L, N_EXPERTS, D), D ** -0.5),
        "v_tab": nrm(ks[22], (L, N_EXPERTS, D), 0.1),
        "normf_w": 1.0 + nrm(ks[23], (D,), 0.02),
    }

def second_block(x, w_in, mu_prev, mu_next, w0, w2, a0, a2, g2, k_k, k_a, r_k, lnx_w, lnx_b,
              q_norm_w, k_norm_w, w_out, norm1_w, norm2_w, w_pq, sub_keys, u_tab, v_tab, normf_w):
    for l in range(DEPTH):
        h = rmsnorm(x, norm1_w[l])
        p = h @ w_in[l]
        z_rwkv, q, k, v = jnp.split(p, IN_SPLITS, axis=-1)
        y_rwkv = rwkv7_bidir(z_rwkv, mu_prev[l], mu_next[l], w0[l], w2[l], a0[l], a2[l], g2[l],
                             k_k[l], k_a[l], r_k[l], lnx_w[l], lnx_b[l]).astype(x.dtype)
        y_attn = axial_gqa(q, k, v, q_norm_w[l], k_norm_w[l])
        x = x + jnp.concatenate([y_rwkv, y_attn], axis=-1) @ w_out[l]
        h2 = rmsnorm(x, norm2_w[l])
        x = x + peer_ffn(h2, w_pq[l], sub_keys[l], u_tab[l], v_tab[l])
    return rmsnorm(x, normf_w)


def setup_inputs(seed=0):
    out = dict(first_inputs(seed))
    for name, value in second_inputs(seed + 1).items():
        if name != "x":
            out[name + "_2"] = value
    return out


def reference(
    x, attn_norm, w_in, sgu_w, sgu_b, conv_w, q_norm, k_norm, w_out, mlp_norm, w_mlp_in,
    w_mlp_out, w_in_2, mu_prev_2, mu_next_2, w0_2, w2_2, a0_2, a2_2, g2_2, k_k_2, k_a_2, r_k_2,
    lnx_w_2, lnx_b_2, q_norm_w_2, k_norm_w_2, w_out_2, norm1_w_2, norm2_w_2, w_pq_2, sub_keys_2,
    u_tab_2, v_tab_2, normf_w_2,
):
    x = first_block(
        x, attn_norm, w_in, sgu_w, sgu_b, conv_w, q_norm, k_norm, w_out, mlp_norm, w_mlp_in,
        w_mlp_out,
    )
    return second_block(
        x, w_in_2, mu_prev_2, mu_next_2, w0_2, w2_2, a0_2, a2_2, g2_2, k_k_2, k_a_2, r_k_2,
        lnx_w_2, lnx_b_2, q_norm_w_2, k_norm_w_2, w_out_2, norm1_w_2, norm2_w_2, w_pq_2,
        sub_keys_2, u_tab_2, v_tab_2, normf_w_2,
    )


_drawn_inputs = setup_inputs


def setup_inputs(seed=0):
    import zlib

    import numpy as np

    out = dict(_drawn_inputs(seed))
    spreads = {}
    factors = {'q_norm': 8.0,
     'k_norm': 8.0,
     'mlp_norm': 3.332,
     'w2_2': 6.513,
     'a0_2': 7.324,
     'lnx_w_2': 64.0,
     'lnx_b_2': 64.0,
     'q_norm_w_2': 23.938,
     'k_norm_w_2': 26.242,
     'norm1_w_2': 6.675,
     'norm2_w_2': 64.0,
     'normf_w_2': 7.742,
     'k_k_2': 3.886}
    for name, (base, spread) in spreads.items():
        noise = np.random.default_rng([zlib.crc32(name.encode()), seed]).standard_normal(out[name].shape)
        drawn = base * np.exp(spread * noise) if base else spread * noise
        out[name] = __import__('jax').numpy.asarray(drawn.astype(out[name].dtype))
    for name, factor in factors.items():
        out[name] = (out[name] * factor).astype(out[name].dtype)
    return out
```

```python
from contextlib import ExitStack

import numpy as np

import concourse.bass as bass
from concourse import mybir
from concourse.alu_op_type import AluOpType as ALU

F32 = mybir.dt.float32
BF16 = mybir.dt.bfloat16
U32 = mybir.dt.uint32
ACT = mybir.ActivationFunctionType
AX = mybir.AxisListType.X

P = 128
T = 256
D = 2048
KD = D // P
HD = 64
EPS = 1e-6
GN_EPS = 64e-5
HALF = 8
BLK = HALF * P
RAW = 28
RING = 4
DECAY = float(np.exp(-0.5))
NEG = -1e30
LOWEST = -3.0e38

STAGES = [("w_in", 44, 2), ("w_out", 16, 2), ("mlp_in", 64, 2), ("mlp_out", 16, 8),
          ("w_in2", 42, 2), ("w_out2", 16, 2), ("w_pq", 16, 2), ("u_tab", 128, 2), ("v_tab", 16, 16)]
UNIT0, BLOCK0 = {}, {}
_u = _b = 0
for _name, _n, _per in STAGES:
    UNIT0[_name] = _u
    BLOCK0[_name] = _b - 88
    _u += _n
    _b += _n * _per
UNITS = {n: u for n, u, _ in STAGES}
PER = {n: p for n, _, p in STAGES}
FP32_BLOCKS = 88

PARAMS = [("attn_norm", 16), ("mlp_norm", 16), ("norm1", 16), ("norm2", 16), ("normf", 16),
          ("conv_w", 18), ("q_norm", 1), ("k_norm", 1), ("q_norm2", 1), ("k_norm2", 1),
          ("mu_prev", 42), ("mu_next", 42), ("w0", 16), ("a0", 16), ("k_k", 8), ("k_a", 8),
          ("r_k", 8), ("lnx_w", 8), ("lnx_b", 8)]
PCOL, _c = {}, 0
for _name, _n in PARAMS:
    PCOL[_name] = _c
    _c += _n
NPAR = _c


def build(nc, A):
    V, S_, PE, G_ = nc.vector, nc.scalar, nc.tensor, nc.gpsimd
    with ExitStack() as ctx:
        def sb(name, words):
            return ctx.enter_context(nc.sbuf_tensor(name, [P, words], F32))

        def sem(name):
            return ctx.enter_context(nc.semaphore(name))

        wring = sb("wring", RING * BLK)
        sring = sb("sring", RING * BLK)
        xT = sb("xT", KD * T)
        hbuf = sb("hbuf", KD * T)
        arena = sb("arena", 32768)
        aux = sb("aux", 2816)
        cst = sb("cst", 4 * P)
        par = sb("par", NPAR)
        c0 = sb("c0", 42)
        ps = ctx.enter_context(nc.psum_tensor("ps", [P, 8, 512], F32))

        wv = wring[:, :].rearrange("p (s k n) -> p s k n", s=RING, k=HALF)
        sv = sring[:, :].bitcast(BF16).rearrange("p (s v k n) -> p s v k n", s=RING, v=2, k=HALF)
        x3 = xT[:, :].rearrange("p (c t) -> p c t", t=T)
        hv = hbuf[:, :].bitcast(BF16).rearrange("p (v c t) -> p v c t", v=2, c=KD)
        h_hi, h_lo = hv[:, 0], hv[:, 1]
        ident, ones, blockones, iota = (cst[:, i * P:(i + 1) * P] for i in range(4))

        def words(base, n, inner=None, buf=arena):
            v = buf[:, base:base + n]
            return v if inner is None else v.rearrange("p (c t) -> p c t", t=inner)

        def col(name, i=0):
            return par[:, PCOL[name] + i:PCOL[name] + i + 1]

        pT = words(0, 44 * T, T)
        yT = words(11264, 4096, T)
        PR = words(15360, 24 * T, T)
        ctmp = words(15360, 6 * T, T)
        zpad = words(16896, 6 * 258, 258)
        hsm, hsr, hsy, hst = (words(15360 + 768 * i, 768)[0:8] for i in range(4))
        dmask = words(21504, 6 * T, T)
        sguw = words(23040, 1024, P)
        sgub = words(24064, 512, P)
        vtok_a = words(24576, 1024, 512)
        vtok_c = words(25600, 1536, 768)
        PTs = words(27136, 768, 384)
        scr = words(28672, 4096, T)
        qk_sq = words(28672, 12 * T, T)
        n_m, n_s, n_y, n_t = (words(i * T, T, buf=aux) for i in range(4))
        n_acc = n_s
        n_sq = words(2 * T, 2 * T, T, buf=aux)
        rl = words(1024, 512, T, buf=aux)
        sqr = words(1536, 512, T, buf=aux)
        sel8 = words(2048, 32, 8, buf=aux)
        selT8 = words(2080, 512, P, buf=aux)[0:8]
        a_mx, a_negm, a_den, a_ln, a_e = (words(2592 + 24 * i, 24, buf=aux) for i in range(5))
        a_M, a_r = words(2712, 8, 4, buf=aux), words(2720, 8, 4, buf=aux)

        def by_pattern(v):
            return v.rearrange("p (q g j) -> p q g j", q=2, g=3)
        hid = arena[:, 0:16384].bitcast(BF16).rearrange("p (v c t) -> p v c t", v=2, c=64)

        pT2 = words(0, 42 * T, T)
        R0, K0, V0, WL, AL, GL, Q0, KK0, VV0 = 0, 8, 16, 24, 26, 28, 30, 38, 40
        AQ = words(10752, 4096).rearrange("p (c k v t) -> p c k v t", c=8, k=4, v=2)
        BG = words(14848, 4096).rearrange("p (c k v t) -> p c k v t", c=8, k=4, v=2)
        lw, LL, EE, aa = (words(18944 + 2048 * i, 2048, T) for i in range(4))
        lora = words(27136, 2048)
        WW = words(18944, 2048).rearrange("p (c o t) -> p c o t", c=8, o=2)
        TR = words(20992, 2048).rearrange("p (s c t) -> p s c t", s=2, c=8)
        MT = words(23040, 1024, P)
        Mc = words(24064, 512, HD)
        Yc = words(24576, 512, HD)
        YY = words(25088, 1024, P)
        RS = words(24576, 512, HD)
        idc = words(32672, 64)
        BGt = words(26112, 1024, P)
        UV = words(27136, 1024, P)
        BD = words(28160, 1024, P)
        YS = words(29184, 2048, T)
        PC = words(31232, 32, 4)
        tail = words(31264, 896)
        wmask = words(31264, 256, P)
        lev = words(31520, 384, 64)
        Tp = words(32160, 512, 64)
        restart = words(31904, 256)
        cosT, sinT, perm = words(31264, 256), words(31520, 256), words(31776, 128)
        ksum = words(0, 2048, T, buf=hbuf)
        PCM = words(2048, 1024, P, buf=hbuf)
        SP_ = words(3072, 1024, P, buf=hbuf)
        kk = words(0, 2048, T, buf=aux)
        hA = [words(21248 + 768 * i, 768)[0:8] for i in range(3)]
        hB = [words(18944 + 768 * i, 768)[0:8] for i in range(3)]
        hK = [words(2048 + 512 * i, 512, buf=hbuf)[0:8] for i in range(3)]

        def factors_of(site):
            return {"gqa": hB, "kk": hK}.get(site, hA)
        kk_sq = words(10752, 2048, T)
        sq2 = words(24064, 2560, T)
        rb = words(0, 2048, T)
        bv = words(25088, 2048, T)
        PR2 = words(10752, 32 * T, T)
        yA = words(18944, 2048, T)
        rtmp = words(26624, 512, T)
        qcos = words(10752, 10 * T, T)
        vtok2 = words(27136, 512, 256)
        PT2 = words(27648, 1024, 512)
        g_negm, g_den = words(2592, 32, buf=aux), words(2624, 32, buf=aux)
        gq8 = words(2656, 1, buf=aux)
        qT2 = words(0, 4096, T)
        skT = words(4096, 2048, P)
        s1 = words(6144, 4096).rearrange("p (u h n) -> p u h n", u=2, h=16)
        s2 = words(10240, 4096).rearrange("p (u h n) -> p u h n", u=2, h=16)
        cand = words(14336, 4096).rearrange("p (u h a b) -> p u h a b", u=2, h=8, a=16)
        cand2 = words(6144, 4096).rearrange("p (u h n) -> p u h n", u=2, h=8)
        topv = words(18432, 512).rearrange("p (u h n) -> p u h n", u=2, h=16)
        topi = words(19456, 512).bitcast(U32).rearrange("p (u h n) -> p u h n", u=2, h=16)
        topif = words(20480, 512).rearrange("p (u h n) -> p u h n", u=2, h=16)
        best = words(21504, 256).rearrange("p (u h n) -> p u h n", u=2, h=8)
        bi = words(21760, 256).bitcast(U32).rearrange("p (u h n) -> p u h n", u=2, h=8)
        ab = words(22016, 512).bitcast(U32)
        abf = words(22528, 512).rearrange("p (v u h n) -> p v u h n", v=2, u=2, h=8)
        e12g = words(23040, 768).rearrange("p (v u n) -> p v u n", v=3, u=2)
        gsum = words(23808, 16, 8)
        big1 = words(10240, 2048).rearrange("p (h n j) -> p h n j", h=8, n=16)
        big2 = words(12288, 2048).rearrange("p (h n j) -> p h n j", h=8, n=16)
        ET = words(0, 768, T, buf=aux)
        OH = words(768, 2048, buf=aux).rearrange("p (s v t n) -> p s v t n", s=4, v=2, t=2)
        gl = words(1792, 512, T, buf=aux)
        gm = words(2304, 512, T, buf=aux)
        gr = words(768, 512, T, buf=aux)
        G3 = words(0, 32768, T)
        Gb = arena[:, :].bitcast(BF16).rearrange("p (e v t) -> p e v t", v=2, t=T)

        w_arrived = [sem(f"w_arrived{i}") for i in range(RING)]
        const_in, mask_in, sguw_in = sem("const_in"), sem("mask_in"), sem("sguw_in")
        x_in = [sem(f"x_in{j}") for j in range(4)]
        f_mm = sem("f_mm")
        hi_done, lo_done = sem("hi_done"), sem("lo_done")
        blk_mm = sem("blk_mm")
        freed = sem("psum_freed")
        dve = sem("dve_chain")
        sq_ready, ms_ready, m_ready, rt_ready = sem("sq_ready"), sem("ms_ready"), sem("m_ready"), sem("rt_ready")
        hf_ready, hhi_ready, h_ready = sem("hf_ready"), sem("hhi_ready"), sem("h_ready")
        tr_ready, tr_freed = sem("vtok_ready"), sem("vtok_copied")
        sq_heads = sem("sq_heads")
        hs_ready, hm_ready, hrt_ready, hr_ready = sem("headsum_ready"), sem("headmean_ready"), sem("headroot_ready"), sem("headrstd_ready")
        bc_ready, bc_used = sem("bcast_ready"), sem("bcast_used")
        sguw_ready, mix_ready, mix_used = sem("sguw_ready"), sem("mix_ready"), sem("mix_used")
        sc_ready, sc_used = sem("scores_ready"), sem("scores_used")
        negm_ready, exp_ready, ln_ready, lse_ready, alpha_ready = sem("negm_ready"), sem("exp_ready"), sem("ln_ready"), sem("lse_ready"), sem("alpha_ready")
        psc_ready = sem("probs_scaled")
        pt_ready, pt_copied, pv_ready = sem("pt_ready"), sem("pt_copied"), sem("pv_ready")
        y_ready, yhi_ready, y_split = sem("y_ready"), sem("yhi_ready"), sem("y_split")
        relu_done, hidhi_done, hid_done = sem("relu_done"), sem("hidhi_done"), sem("hid_done")
        out_done = sem("out_done")
        Y_WAITS = [(2, 2, 4, 8), (9, 9, 12, 16)]
        z_scaled, z_prev = sem("z_scaled"), sem("z_prev")
        lora_in, mask2_in, rope_in, sk_in = sem("lora_in"), sem("mask2_in"), sem("rope_in"), sem("subkeys_in")
        kk0_ready, lin_ready = sem("kk0_ready"), sem("lora_inputs_ready")
        zl_ready, zl_used = sem("lora_sums_ready"), sem("lora_sums_used")
        L_ready, e_ready, e_used, prep_done = sem("logdecay_ready"), sem("decay_ready"), sem("decay_used"), sem("prep_done")
        ws_ready, w_done = sem("pair_products_ready"), sem("pair_products_masked")
        bt_ready, bt_copied, vt_ready, vt_copied = sem("bg_transposed"), sem("bg_copied"), sem("v_transposed"), sem("v_copied")
        t_done, nt0, n0_ready, n0_done = sem("level_masked"), sem("inverseT_begun"), sem("inverse_begun"), sem("inverse_begun_copied")
        x_ready, yt_done, yb_done = sem("level_product"), sem("level_factor"), sem("level_factor_diagonal")
        m_mm, mt_mm, mc_done, mt_done, idc_ready = sem("inverse_ready"), sem("inverseT_ready"), sem("inverse_copied"), sem("inverseT_copied"), sem("identities")
        sp_done, r_ready, rs_done, u_ready, u_done = sem("state_decayed"), sem("rhs_ready"), sem("rhs_copied"), sem("u_ready"), sem("u_copied")
        dl_ready, ym_ready, bd_done, yg_done = sem("state_sums"), sem("out_sums"), sem("state_done"), sem("out_copied")
        rb_ready, rope_done, v2_ready, v2_copied = sem("bonus_terms"), sem("rope_done"), sem("v2_ready"), sem("v2_copied")
        g_sc, g_max, g_exp, g_psc = sem("gqa_scores"), sem("gqa_max"), sem("gqa_exp"), sem("gqa_scaled")
        g_pt, g_ptc, g_pv = sem("gqa_pt"), sem("gqa_pt_copied"), sem("gqa_pv")
        ks_ready, ks_copied, gd_ready, ge_ready = sem("key_scores"), sem("key_scores_copied"), sem("gate_diff"), sem("gate_exp")
        slots_ready, slotsT, et_done = sem("slots_ready"), sem("slots_transposed"), sem("slots_copied")
        oh_ready, ohg_ready, raw_gated, raw_out, raw_hi, raw_done = sem("onehots_ready"), sem("onehots_gated"), sem("raw_gated"), sem("raw_out"), sem("raw_hi"), sem("raw_done")
        g_mm, g_out, gm_done = sem("gates_ready"), sem("gates_copied"), sem("gated")
        dl_used, cos_done, sq_added = sem("state_sums_used"), sem("cosine_part"), sem("norm_squares_added")
        q_done = sem("decayed_r_ready")
        acc0, sq_chunk, acc_done = sem("norm_sum_zeroed"), sem("norm_squares"), sem("norm_sum")
        tp_ready, tp_done, tr0 = sem("triangles_ready"), sem("triangles_masked"), sem("levels_zeroed")
        bd0, pcm_done = sem("state_zeroed"), sem("chunk_decay_spread")
        SITES = ["qk", "kk", "mean", "gqa", "rope", "var", "bonus", "gate"]
        BANKS = {"qk": 6, "kk": 4, "mean": 4, "var": 4, "bonus": 4, "gate": 4, "gqa": 5, "rope": 5}
        SUMS = ["qk", "kk", "mean", "gqa", "var", "bonus"]
        ROOTS = ["qk", "kk", "gqa", "var"]

        def banks_before(site):
            return sum(BANKS[x] for x in SITES[:SITES.index(site)])

        def time_chunk(g):
            return g if g < 4 else 7 - g
        block = ctx.enter_context(nc.Block())

        def stage_done(name):
            return UNIT0[name] + UNITS[name]

        def for_units(e, name, make_part, take_out, first=0, stop=None):
            n, per = UNITS[name], PER[name]
            end = stop or n

            def pair(i, last):
                for r in range(2):
                    for j in range(per):
                        if not (last and per * r + RING + j >= 2 * per):
                            make_part(i, per * r + RING + j, (per * r + j) % RING)
                    take_out(2 * i + r, r)

            with e.Fori(first // 2, end // 2 - 1) as i:
                pair(i, False)
            pair(end // 2 - 1, end == n)

        def lo_part(e, E, name):
            b0, per = BLOCK0[name], PER[name]

            def make(i, k, slot):
                e.wait_ge(hi_done, 2 * per * i + (b0 + k + 1))
                E.tensor_tensor(sv[:, slot, 1], wv[:, slot], sv[:, slot, 0], ALU.subtract).then_inc(lo_done, 1)
            return make

        @block.sync
        def _(sp):
            for j in range(4):
                sp.dma_start(xT[:, 4 * j * T:(4 * j + 4) * T], A["x"][:, 4 * j * T:(4 * j + 4) * T]).then_inc(x_in[j], 16)
            sp.dma_start(cst[:, :], A["cst_main"]).then_inc(const_in, 16)
            sp.dma_start(par[:, :], A["params"]).then_inc(const_in, 16)

            def load(src, s, slot):
                sp.dma_start(wring[:, slot * BLK:(slot + 1) * BLK], src[s]).then_inc(w_arrived[slot], 16)

            w = A["w_in"]
            sp.wait_ge(x_in[3], 16)
            for s in range(RING):
                load(w, s, s)
            with sp.Fori(1, FP32_BLOCKS // RING) as i:
                for p in range(RING):
                    sp.wait_ge(f_mm, RING * i + (p - RING + 1))
                    load(w, RING * i + p, p)
            for name, units, per in STAGES[1:]:
                b0, w = BLOCK0[name], A[name]
                first = 0
                if name == "w_out":
                    first = 1
                    for s in range(RING):
                        sp.wait_ge(f_mm, FP32_BLOCKS - RING + s + 1)
                        load(w, s, s)
                with sp.Fori(first, units * per // RING) as i:
                    for p in range(RING):
                        sp.wait_ge(lo_done, RING * i + (b0 + p - RING + 1))
                        load(w, RING * i + p, p)

        @block.scalar
        def _(act):
            def hi_part(name):
                b0, per = BLOCK0[name], PER[name]

                def make(i, k, slot):
                    act.wait_ge(w_arrived[slot], (16 * 2 * per // RING) * i + 16 * (FP32_BLOCKS + b0 + k - slot) // RING + 16)
                    if b0 + k >= RING or not isinstance(i, int):
                        act.wait_ge(blk_mm, 2 * per * i + (b0 + k - RING + 1))
                    S_.activation(sv[:, slot, 0], wv[:, slot], ACT.Copy).then_inc(hi_done, 1)
                return make

            def ahead(name):
                for k in range(RING):
                    hi_part(name)(0, k, k)

            def norm(n):
                if n == 0:
                    for j in range(4):
                        act.wait_ge(x_in[j], 16)
                        S_.activation(scr[:, 4 * j:4 * j + 4], x3[:, 4 * j:4 * j + 4], ACT.Square).then_inc(sq_ready, 1)
                act.wait_ge(m_ready, n + 1)
                S_.activation(n_s, n_m, ACT.Abs_reciprocal_sqrt).then_inc(rt_ready, 1)
                if n in (1, 2, 3):
                    for j in range(4):
                        act.wait_ge(hf_ready, 4 * n + j + 1)
                        S_.activation(h_hi[:, 4 * j:4 * j + 4], scr[:, 4 * j:4 * j + 4], ACT.Copy).then_inc(hhi_ready, 1)

            def split_hi(n, groups):
                for j in range(4):
                    act.wait_ge(y_ready, Y_WAITS[n][j])
                    S_.activation(h_hi[:, 4 * j:4 * j + 4], groups[j], ACT.Copy).then_inc(yhi_ready, 1)

            norm(0)
            act.dma_start(words(21504, 1536), A["dmask"]).then_inc(mask_in, 16)
            act.dma_start(words(23040, 1024), A["sgu_w"]).then_inc(sguw_in, 16)
            act.dma_start(words(24064, 512), A["sgu_b"]).then_inc(mask_in, 16)
            act.dma_start(words(2048, 544, buf=aux), A["cst_sel"]).then_inc(mask_in, 16)
            S_.preload_act_table(ACT.Copy)
            with act.Fori(0, UNITS["w_in"] // 2) as i:
                for r in range(2):
                    act.wait_ge(f_mm, 4 * i + (2 * r + 2))
                    S_.activation(pT[:, 2 * i + r], ps[:, r, 0:T], ACT.Copy).then_inc(freed, 1)
            act.wait_ge(freed, 44)
            S_.activation(qk_sq, pT[:, 26:38], ACT.Square).then_inc(sq_heads, 1)
            for tt in range(2):
                act.wait_ge(tr_ready, tt + 1)
                S_.activation(vtok_a[:, tt], ps[:, 2 + tt, :], ACT.Copy).then_inc(tr_freed, 1)
            for tt in range(2):
                act.wait_ge(tr_ready, 3 + tt)
                S_.activation(vtok_c[:, tt, 0:512], ps[:, 4 + 2 * tt, :], ACT.Copy).then_inc(tr_freed, 1)
                S_.activation(vtok_c[:, tt, 512:768], ps[:, 5 + 2 * tt, 0:256], ACT.Copy).then_inc(tr_freed, 1)
            ahead("w_out")
            act.wait_ge(hm_ready, 1)
            S_.activation(hsr, hsm, ACT.Abs_reciprocal_sqrt).then_inc(hrt_ready, 1)
            for n in range(24):
                hd, qt = n // 2, n % 2
                if n % 4 == 0:
                    act.wait_ge(negm_ready, n // 4 + 1)
                c = qt * 12 + hd
                S_.activation(PR[:, n, 0:P * (qt + 1)], PR[:, n, 0:P * (qt + 1)], ACT.Exp, bias=a_negm[:, c:c + 1],
                              accum_out=a_den[:, c:c + 1]).then_inc(exp_ready, 1)
            act.wait_ge(exp_ready, 24)
            S_.activation(a_ln, a_den, ACT.Ln).then_inc(ln_ready, 1)
            act.wait_ge(lse_ready, 1)
            S_.activation(a_e, a_e, ACT.Exp).then_inc(alpha_ready, 1)
            for hd in range(12):
                act.wait_ge(pt_ready, hd + 1)
                if hd >= 2:
                    act.wait_ge(pv_ready, hd - 1)
                S_.activation(PTs[:, hd % 2], ps[:, 2 + hd % 2, 0:384], ACT.Copy).then_inc(pt_copied, 1)
            split_hi(0, [yT[:, 4 * j:4 * j + 4] for j in range(4)])
            for_units(act, "w_out", hi_part("w_out"), lambda u, r: None)
            ahead("mlp_in")
            norm(1)

            def relu(u, r):
                act.wait_ge(blk_mm, 2 * u + (BLOCK0["mlp_in"] + 2))
                act.wait_ge(freed, u + (UNIT0["mlp_in"] - 1))
                S_.activation(rl[:, r], ps[:, r, 0:T], ACT.Relu).then_inc(relu_done, 1)
            S_.preload_act_table(ACT.Relu)
            for_units(act, "mlp_in", hi_part("mlp_in"), relu)
            ahead("mlp_out")
            for_units(act, "mlp_out", hi_part("mlp_out"), lambda u, r: None)
            ahead("w_in2")
            norm(2)
            act.wait_ge(h_ready, 8)
            act.dma_start(tail, A["cst_rw"]).then_inc(mask2_in, 16)
            act.dma_start(lora, A["lora"][0]).then_inc(lora_in, 16)

            def scale_z(u, r):
                act.wait_ge(blk_mm, 2 * u + (BLOCK0["w_in2"] + 2))
                S_.activation(pT2[:, u], ps[:, r, 0:T], ACT.Copy, scale=c0[:, bass.ds(u, 1)]).then_inc(z_scaled, 1)
            S_.preload_act_table(ACT.Copy)
            for_units(act, "w_in2", hi_part("w_in2"), scale_z)
            ahead("w_out2")
            act.wait_ge(freed, stage_done("w_in2"))
            S_.activation(pT2[:, WL:WL + 2], pT2[:, WL:WL + 2], ACT.Tanh).then_inc(lin_ready, 1)
            S_.activation(pT2[:, GL:GL + 2], pT2[:, GL:GL + 2], ACT.Sigmoid).then_inc(lin_ready, 1)

            def root(site, n):
                act.wait_ge(hm_ready, ROOTS.index(site) + 1)
                h = factors_of(site)
                S_.activation(h[1][:, 0:n], h[0][:, 0:n], ACT.Abs_reciprocal_sqrt).then_inc(hrt_ready, 1)

            act.wait_ge(kk0_ready, 1)
            S_.activation(kk_sq, kk, ACT.Square).then_inc(sq_heads, 1)
            for d in range(2):
                if d == 1:
                    act.wait_ge(bd_done, 4)
                    act.wait_ge(yg_done, 4)
                    act.dma_start(lora, A["lora"][1]).then_inc(lora_in, 16)
                for c in range(8):
                    act.wait_ge(zl_ready, 8 * d + c // 2 + 1)
                    S_.activation(lw[:, c], ps[:, c // 2, (c % 2) * T:(c % 2 + 1) * T], ACT.Sigmoid, bias=col("w0", 8 * d + c)).then_inc(zl_used, 1)
                for c in range(8):
                    act.wait_ge(zl_ready, 8 * d + 4 + c // 2 + 1)
                    S_.activation(aa[:, c], ps[:, 4 + c // 2, (c % 2) * T:(c % 2 + 1) * T], ACT.Sigmoid, bias=col("a0", 8 * d + c)).then_inc(zl_used, 1)
                if d == 0:
                    root("kk", 512)
                act.wait_ge(L_ready, d + 1)
                S_.activation(EE, lw, ACT.Exp, scale=-DECAY).then_inc(e_ready, 1)
                act.wait_ge(e_ready, 3 * d + 1)
                S_.activation(lw, LL, ACT.Exp, scale=DECAY).then_inc(e_ready, 1)
                act.wait_ge(e_used, d + 1)
                S_.activation(EE, LL, ACT.Exp, scale=-DECAY)
                S_.activation(PC, PC, ACT.Exp, scale=-DECAY).then_inc(e_ready, 1)
                for g in range(4 * d, 4 * d + 4):
                    for n, what in enumerate(("v0", "bg1", "bg0", "v1")):
                        j = int(what[-1])
                        if what[0] == "v":
                            act.wait_ge(vt_ready, 2 * g + j + 1)
                            S_.activation(UV[64:128, 4 * j:4 * j + 4], ps[64:128, 6 + j, :].rearrange("p (c t) -> p c t", t=P), ACT.Copy).then_inc(vt_copied, 1)
                        else:
                            act.wait_ge(bt_ready, 2 * g + n)
                            S_.activation(BGt[:, 4 * j:4 * j + 4], ps[:, 4 + j, :].rearrange("p (c t) -> p c t", t=P), ACT.Copy).then_inc(bt_copied, 1)
                    for j in range(2):
                        act.wait_ge(n0_ready, 2 * g + j + 1)
                        S_.activation(Mc[:, 4 * j:4 * j + 4], ps[:, j, 0:T].rearrange("p (c t) -> p c t", t=HD), ACT.Copy).then_inc(n0_done, 1)
                    for l in range(5):
                        if l < 4:
                            for j in range(2):
                                act.wait_ge(m_mm, 8 * g + 2 * l + j + 1)
                                S_.activation(Mc[:, 4 * j:4 * j + 4], ps[:, 2 + j, 0:T].rearrange("p (c t) -> p c t", t=HD), ACT.Copy).then_inc(mc_done, 1)
                        for j in range(2):
                            act.wait_ge(mt_mm, 10 * g + 2 * l + j + 1)
                            S_.activation(MT[:, 4 * j:4 * j + 4], ps[:, 4 + j, :].rearrange("p (c t) -> p c t", t=P), ACT.Copy).then_inc(mt_done, 1)
                    for j in range(2):
                        act.wait_ge(r_ready, 2 * g + j + 1)
                        S_.activation(RS[:, 4 * j:4 * j + 4], ps[:, 6 + j, 0:T].rearrange("p (c t) -> p c t", t=HD), ACT.Copy, scale=-1.0).then_inc(rs_done, 1)
            act.wait_ge(yg_done, 8)
            act.wait_ge(bd_done, 8)
            act.dma_start(lora, A["gate_w"]).then_inc(lora_in, 16)
            act.dma_start(words(31264, 640), A["cst_rope"]).then_inc(rope_in, 16)
            S_.activation(sq2[:, 0:10], pT2[:, Q0:Q0 + 10], ACT.Square).then_inc(sq_heads, 1)
            root("gqa", 768)
            act.wait_ge(bc_used, banks_before("gqa"))
            S_.activation(sq2[:, 0:8], YS, ACT.Square).then_inc(sq_heads, 1)
            root("var", 512)
            act.wait_ge(v2_ready, 1)
            S_.activation(vtok2, ps[:, 7, :].rearrange("p (u n) -> p u n", u=2), ACT.Copy).then_inc(v2_copied, 1)

            def probabilities(pc):
                for m in range(4 * pc, 4 * pc + 4):
                    q, odd = m // 2, m % 2
                    act.wait_ge(g_max, m + 1)
                    S_.activation(PR2[:, m], ps[:, 4 + odd + 2 * (q % 2), 0:T], ACT.Exp, bias=g_negm[:, m:m + 1], accum_out=g_den[:, m:m + 1]).then_inc(g_exp, 1)

            probabilities(0)
            probabilities(1)
            for pc in range(8):
                for odd in range(2):
                    act.wait_ge(g_pt, 2 * pc + odd + 1)
                    S_.activation(PT2[:, odd], ps[:, odd, :], ACT.Copy).then_inc(g_ptc, 1)
                if pc < 6:
                    probabilities(pc + 2)
            split_hi(1, [YS[:, 0:4], YS[:, 4:8], yA[:, 0:4], yA[:, 4:8]])
            act.wait_ge(y_split, 8)
            act.dma_start(skT, A["subkeys"].rearrange("p (h n) -> p h n", n=P)).then_inc(sk_in, 16)
            for_units(act, "w_out2", hi_part("w_out2"), lambda u, r: None)
            ahead("w_pq")
            norm(3)

            def copy_q(u, r):
                act.wait_ge(blk_mm, 2 * u + (BLOCK0["w_pq"] + 2))
                S_.activation(qT2[:, u], ps[:, r, 0:T], ACT.Copy).then_inc(freed, 1)
            S_.preload_act_table(ACT.Copy)
            for_units(act, "w_pq", hi_part("w_pq"), copy_q)
            ahead("u_tab")
            for j in range(8):
                act.wait_ge(ks_ready, j + 1)
                S_.activation(s1[:, j // 4, 4 * (j % 4):4 * (j % 4) + 4], ps[:, (2 + j) % 8, :].rearrange("p (h n) -> p h n", n=P), ACT.Copy).then_inc(ks_copied, 1)

            def gelu_raw(u, r):
                act.wait_ge(blk_mm, 2 * u + (BLOCK0["u_tab"] + 2))
                S_.activation(G3[:, u + (P - RAW)], ps[:, r, 0:T], ACT.Gelu).then_inc(freed, 1)
            S_.preload_act_table(ACT.Gelu)
            for_units(act, "u_tab", hi_part("u_tab"), gelu_raw, 0, RAW)
            act.wait_ge(gd_ready, 1)
            S_.activation(e12g[:, 2], e12g[:, 2], ACT.Exp).then_inc(ge_ready, 1)
            act.wait_ge(slotsT, 1)
            S_.activation(ET[:, 0:2], ps[:, 2, :].rearrange("p (v t) -> p v t", v=2), ACT.Copy).then_inc(et_done, 1)
            S_.activation(ET[:, 2], ps[:, 3, 0:T], ACT.Copy).then_inc(et_done, 1)
            S_.preload_act_table(ACT.Copy)
            with act.Fori(0, T // 16) as i:
                for r in range(8):
                    act.wait_ge(g_mm, 8 * i + (r + 1))
                    S_.activation(G3[:, 0:P - RAW, bass.ds(16 * i + 2 * r, 2)], ps[:, 2 + r % 4, 0:T].rearrange("p (t e) -> p e t", t=2)[:, 0:P - RAW], ACT.Copy).then_inc(g_out, 1)

            def gelu(u, r):
                act.wait_ge(blk_mm, 2 * u + (BLOCK0["u_tab"] + 2))
                act.wait_ge(hidhi_done, u + (63 - RAW))
                S_.activation(gl[:, r], ps[:, r, 0:T], ACT.Gelu).then_inc(freed, 1)
            S_.preload_act_table(ACT.Gelu)
            for_units(act, "u_tab", hi_part("u_tab"), gelu, RAW)
            ahead("v_tab")
            for_units(act, "v_tab", hi_part("v_tab"), lambda u, r: None)
            norm(4)
            for j in range(4):
                act.wait_ge(hf_ready, 17 + j)
                act.dma_start(A["out"][:, 4 * j * T:(4 * j + 4) * T], words(28672 + 4 * j * T, 4 * T)).then_inc(out_done, 16)
            act.wait_ge(out_done, 64)

        @block.gpsimd
        def _(pool):
            pool.wait_ge(sguw_in, 16)
            G_.affine_select(out=sguw, in_=sguw, compare_op=ALU.is_ge, fill=0.0, base=0,
                             pattern=[[0, 8], [1, P]], channel_multiplier=-1).then_inc(sguw_ready, 1)

            def squares(n, name):
                u0, b = UNIT0[name], KD * (n - 1)
                pool.wait_ge(hf_ready, 4 * n)
                G_.memset(n_acc, 0.0).then_inc(acc0, 1)
                pool.wait_ge(acc0, n)
                with pool.Fori(0, KD // 2) as i:
                    for r in range(2):
                        pool.wait_ge(freed, 2 * i + (u0 + r + 1))
                        G_.tensor_tensor(n_sq[:, r], x3[:, 2 * i + r], x3[:, 2 * i + r], ALU.mult).then_inc(sq_chunk, 1)
                        pool.wait_ge(sq_chunk, 2 * i + (b + r + 1))
                        if n > 1 or r:
                            pool.wait_ge(acc_done, 2 * i + (b + r))
                        G_.tensor_tensor(n_acc, n_acc, n_sq[:, r], ALU.add).then_inc(acc_done, 1)
            squares(1, "w_out")
            squares(2, "mlp_out")
            for g in range(8):
                d, k = g // 4, time_chunk(g)
                if g:
                    pool.wait_ge(t_done, 12 * g)
                if g % 4 == 0:
                    pool.wait_ge(e_ready, 3 * d + 3)
                    G_.tensor_tensor(AQ[:, :, :, 1].rearrange("p c k t -> p (c k) t"), pT2[:, R0:R0 + 8].rearrange("p c (k t) -> p (c k) t", t=64),
                                     EE.rearrange("p c (k t) -> p (c k) t", t=64), ALU.mult).then_inc(q_done, 1)
                    pool.wait_ge(mask2_in, 16)
                    G_.memset(TR, 0.0).then_inc(tr0, 1)
                    pool.wait_ge(prep_done, d + 1)
                    G_.memset(YY, 0.0).then_inc(tr0, 1)
                for l in range(6):
                    if l == 0:
                        pool.wait_ge(tp_done, g + 1)
                        pool.wait_ge(tr0, 2 * d + 2)
                    if l == 2:
                        pool.wait_ge(t_done, 12 * g + 4)
                        if g % 4 == 0:
                            G_.memset(BD, 0.0).then_inc(bd0, 1)
                            pool.wait_ge(bd0, d + 1)
                        else:
                            pool.wait_ge(bd_done, g)
                        G_.tensor_tensor(PCM, PC[:, :, k].unsqueeze(2).to_broadcast([P, 8, P]), blockones.unsqueeze(1).to_broadcast([P, 8, P]), ALU.mult).then_inc(pcm_done, 1)
                        pool.wait_ge(pcm_done, g + 1)
                        G_.tensor_tensor(SP_, BD, PCM, ALU.mult).then_inc(sp_done, 1)
                        pool.wait_ge(sp_done, g + 1)
                        pool.wait_ge(nt0, g + 1)
                    if l > 2:
                        pool.wait_ge(x_ready, 10 * g + 2 * (l - 2))
                    for odd in range(2):
                        b = HD * odd
                        if l or odd:
                            pool.wait_ge(t_done, 12 * g + 2 * l + odd)
                        G_.tensor_tensor(TR[b:b + HD, l % 2, :, b:b + HD], Tp[b:b + HD], lev[b:b + HD, l].unsqueeze(1).to_broadcast([HD, 8, HD]), ALU.mult).then_inc(t_done, 1)
            pool.wait_ge(t_done, 96)
            pool.wait_ge(rope_in, 16)
            pool.wait_ge(bc_used, banks_before("rope"))
            G_.tensor_tensor(qcos, pT2[:, Q0:Q0 + 10], cosT.unsqueeze(1).to_broadcast([P, 10, T]), ALU.mult).then_inc(cos_done, 1)
            squares(3, "w_out2")
            for k in range(RING):
                lo_part(pool, G_, "u_tab")(0, k, k)
            for_units(pool, "u_tab", lo_part(pool, G_, "u_tab"), lambda u, r: None, 0, RAW)
            with pool.Fori(0, T // 16) as i:
                for r in range(8):
                    pool.wait_ge(oh_ready, 8 * i + (r + 1))
                    G_.tensor_tensor(OH[:, r % 4, 1], OH[:, r % 4, 1], ET[:, 2, bass.ds(16 * i + 2 * r, 2)].unsqueeze(2).to_broadcast([P, 2, P]), ALU.mult).then_inc(ohg_ready, 1)
            pool.wait_ge(hid_done, 64 + P - RAW)
            squares(4, "v_tab")

        @block.vector
        def _(v):
            chain = [0]

            def link(ins):
                chain[0] += 1
                ins.then_inc(dve, 1)
                v.wait_ge(dve, chain[0])

            def ahead(name):
                for k in range(RING):
                    lo_part(v, V, name)(0, k, k)

            def rsqrt(y, m, y0, t, last):
                link(V.scalar_tensor_tensor(t, y0, -0.5, y0, ALU.mult, ALU.mult))
                link(V.tensor_tensor(t, t, m, ALU.mult))
                ins = V.scalar_tensor_tensor(y, t, 1.5, y0, ALU.add, ALU.mult)
                link(ins) if last is None else ins.then_inc(last, 1)

            def norm(n, gain):
                v.wait_ge(ms_ready, n + 1)
                V.tensor_scalar(n_m, ps[:, 7, 0:T], 1.0 / D, EPS, ALU.mult, ALU.add).then_inc(m_ready, 1)
                v.wait_ge(rt_ready, n + 1)
                rsqrt(n_y, n_m, n_s, n_t, None)
                for j in range(5):
                    if j < 4:
                        for c in range(4 * j, 4 * j + 4):
                            ins = V.scalar_tensor_tensor(scr[:, c], x3[:, c], col(gain, c), n_y, ALU.mult, ALU.mult)
                        ins.then_inc(hf_ready, 1)
                    if n in (1, 2, 3) and j:
                        v.wait_ge(hhi_ready, 4 * (n - 1) + j)
                        V.tensor_tensor(h_lo[:, 4 * j - 4:4 * j], scr[:, 4 * j - 4:4 * j], h_hi[:, 4 * j - 4:4 * j],
                                        ALU.subtract).then_inc(h_ready, 1)

            def split_lo(n, groups):
                for j in range(4):
                    v.wait_ge(yhi_ready, 4 * n + j + 1)
                    V.tensor_tensor(h_lo[:, 4 * j:4 * j + 4], groups[j], h_hi[:, 4 * j:4 * j + 4], ALU.subtract).then_inc(y_split, 1)

            def add_to_x(name):
                def take(u, r):
                    v.wait_ge(blk_mm, PER[name] * u + (BLOCK0[name] + PER[name]))
                    V.tensor_tensor(x3[:, u], x3[:, u], ps[:, r, 0:T], ALU.add).then_inc(freed, 1)
                return take

            v.wait_ge(const_in, 32)
            for j in range(4):
                v.wait_ge(x_in[j], 16)
            link(V.tensor_tensor(c0[:, :], par[:, PCOL["mu_prev"]:PCOL["mu_prev"] + 42], par[:, PCOL["mu_next"]:PCOL["mu_next"] + 42], ALU.add))
            link(V.tensor_scalar(c0[:, :], c0[:, :], -1.0, 1.0, ALU.mult, ALU.add))
            for n, (w, at) in enumerate(((4, 4), (4, 8), (4, 12), (2, 2), (1, 1))):
                if n < 3:
                    v.wait_ge(sq_ready, n + 2)
                if n:
                    v.wait_ge(sq_added, n)
                V.tensor_tensor(scr[:, 0:w], scr[:, 0:w], scr[:, at:at + w], ALU.add).then_inc(sq_added, 1)
            norm(0, "attn_norm")
            V.memset(zpad[:, :, 0:2], 0.0)
            v.wait_ge(freed, 26)
            link(V.tensor_tensor(zpad[:, :, 2:258], pT[:, 14:20], pT[:, 20:26], ALU.mult))
            for tap in range(3):
                for c in range(6):
                    w = col("conv_w", 6 * tap + c)
                    if tap == 0:
                        ins = V.tensor_scalar(ctmp[:, c], zpad[:, c, 0:T], w, None, ALU.mult)
                    else:
                        ins = V.scalar_tensor_tensor(ctmp[:, c], zpad[:, c, tap:tap + T], w, ctmp[:, c], ALU.mult, ALU.add)
                    if c == 5:
                        link(ins)
            link(V.tensor_tensor(yT[:, 4:10], ctmp, pT[:, 8:14], ALU.mult))
            v.wait_ge(mask_in, 48)
            for n in range(2):
                v.wait_ge(mix_ready, n + 1)
                t3 = ctmp[:, 0:2].rearrange("p c t -> p (c t)").rearrange("p (c t) -> p c t", t=P)
                link(V.tensor_tensor(t3, ps[:, 2 + n, :].rearrange("p (c t) -> p c t", t=P), sgub, ALU.add))
                V.tensor_tensor(yT[:, 0:4, n * P:(n + 1) * P], t3, pT[:, 0:4, n * P:(n + 1) * P], ALU.mult).then_inc(y_ready, 1)
                v.wait_ge(y_ready, n + 1)
            v.wait_ge(hs_ready, 1)
            V.tensor_scalar(hsm[:, 0:512], ps[0:8, 0, :], 1.0 / HD, EPS, ALU.mult, ALU.add)
            V.tensor_scalar(hsm[:, 512:768], ps[0:8, 1, 0:256], 1.0 / HD, EPS, ALU.mult, ALU.add).then_inc(hm_ready, 1)
            v.wait_ge(hrt_ready, 1)
            rsqrt(hsy, hsm, hsr, hst, hr_ready)
            for j in range(6):
                v.wait_ge(bc_ready, j + 1)
                V.scalar_tensor_tensor(pT[:, 26 + 2 * j:28 + 2 * j], pT[:, 26 + 2 * j:28 + 2 * j], col("q_norm" if j < 3 else "k_norm"),
                                       ps[:, (4 + j) % 8, :].rearrange("p (c t) -> p c t", t=T), ALU.mult, ALU.mult).then_inc(bc_used, 1)
            v.wait_ge(bc_used, 6)
            for m in range(24):
                q, odd = m // 2, m % 2
                hd, qt = 2 * (q // 2) + odd, q % 2
                c, w = qt * 12 + hd, P * (qt + 1)
                v.wait_ge(sc_ready, m + 1)
                V.tensor_tensor_reduce(out=PR[:, 2 * hd + qt, 0:w], in0=ps[:, 2 + odd + 2 * (q % 3), 0:w], in1=dmask[:, 2 * (hd // 4) + qt, 0:w],
                                       scale=HD ** -0.5, scalar=LOWEST, op0=ALU.add, op1=ALU.max, accum_out=a_mx[:, c:c + 1]).then_inc(sc_used, 1)
                if m % 4 == 3:
                    v.wait_ge(sc_used, m + 1)
                    h = hd - 1
                    V.tensor_scalar(a_negm.rearrange("p (q h) -> p q h", q=2)[:, :, h:h + 2], a_mx.rearrange("p (q h) -> p q h", q=2)[:, :, h:h + 2],
                                    -1.0, None, ALU.mult).then_inc(negm_ready, 1)
            ahead("w_out")
            v.wait_ge(ln_ready, 1)
            link(V.tensor_tensor(a_ln, a_ln, a_mx, ALU.add))
            lse = by_pattern(a_ln)
            link(V.tensor_tensor(a_M, lse[:, :, 0], lse[:, :, 1], ALU.max))
            link(V.tensor_tensor(a_M, a_M, lse[:, :, 2], ALU.max))
            V.tensor_tensor(by_pattern(a_e), lse, a_M.unsqueeze(2).to_broadcast([P, 2, 3, 4]), ALU.subtract).then_inc(lse_ready, 1)
            link(V.reciprocal(a_den, a_den))
            v.wait_ge(alpha_ready, 1)
            ae = by_pattern(a_e)
            link(V.tensor_tensor(a_M, ae[:, :, 0], ae[:, :, 1], ALU.add))
            link(V.tensor_tensor(a_M, a_M, ae[:, :, 2], ALU.add))
            link(V.reciprocal(a_r, a_M))
            link(V.tensor_tensor(a_e, a_e, a_den, ALU.mult))
            link(V.tensor_tensor(ae, ae, a_r.unsqueeze(2).to_broadcast([P, 2, 3, 4]), ALU.mult))
            for hd in range(12):
                for qt in range(2):
                    n, c, w = 2 * hd + qt, qt * 12 + hd, P * (qt + 1)
                    ins = V.tensor_scalar(PR[:, n, 0:w], PR[:, n, 0:w], a_e[:, c:c + 1], None, ALU.mult)
                ins.then_inc(psc_ready, 1)
            for pair in range(6):
                v.wait_ge(pv_ready, 2 * pair + 2)
                V.tensor_copy(yT[:, 10 + pair], ps[:, 4 + pair % 2, 0:T]).then_inc(y_ready, 1)
            v.wait_ge(y_ready, 8)
            split_lo(0, [yT[:, 4 * j:4 * j + 4] for j in range(4)])
            for_units(v, "w_out", lo_part(v, V, "w_out"), add_to_x("w_out"))
            ahead("mlp_in")
            v.wait_ge(freed, stage_done("w_out"))
            norm(1, "mlp_norm")

            def square(u, r):
                v.wait_ge(relu_done, u + 1)
                V.scalar_tensor_tensor(sqr[:, r], ps[:, r, 0:T], 0.0, rl[:, r], ALU.max, ALU.mult).then_inc(freed, 1)
                v.wait_ge(freed, u + (UNIT0["mlp_in"] + 1))
                V.tensor_copy(hid[:, 0, u], sqr[:, r]).then_inc(hidhi_done, 1)
                v.wait_ge(hidhi_done, u + 1)
                V.tensor_tensor(hid[:, 1, u], sqr[:, r], hid[:, 0, u], ALU.subtract).then_inc(hid_done, 1)
            for_units(v, "mlp_in", lo_part(v, V, "mlp_in"), square)
            ahead("mlp_out")
            for_units(v, "mlp_out", lo_part(v, V, "mlp_out"), add_to_x("mlp_out"))
            ahead("w_in2")
            v.wait_ge(freed, stage_done("mlp_out"))
            norm(2, "norm1")

            def shift_z(u, r):
                v.wait_ge(z_scaled, u + 1)
                V.scalar_tensor_tensor(pT2[:, u, 1:T], ps[:, r, 0:T - 1], par[:, bass.ds(u + PCOL["mu_prev"], 1)],
                                       pT2[:, u, 1:T], ALU.mult, ALU.add).then_inc(z_prev, 1)
                v.wait_ge(z_prev, u + 1)
                V.scalar_tensor_tensor(pT2[:, u, 0:T - 1], ps[:, r, 1:T], par[:, bass.ds(u + PCOL["mu_next"], 1)],
                                       pT2[:, u, 0:T - 1], ALU.mult, ALU.add).then_inc(freed, 1)
            for_units(v, "w_in2", lo_part(v, V, "w_in2"), shift_z)
            ahead("w_out2")
            v.wait_ge(freed, stage_done("w_in2"))
            link(V.tensor_scalar(gq8, col("q_norm2"), HD ** -0.5, None, ALU.mult))

            def from_banks(site, n, fn):
                b = banks_before(site)
                for j in range(n):
                    v.wait_ge(bc_ready, b + j + 1)
                    fn(j, ps[:, 2 + j, :].rearrange("p (c t) -> p c t", t=T)).then_inc(bc_used, 1)
                v.wait_ge(bc_used, b + n)

            def head_sums(site, n, scale, add):
                v.wait_ge(hs_ready, SUMS.index(site) + 1)
                h = factors_of(site)
                dst = h[0 if site in ROOTS else 2]
                sem_, op = (hm_ready, ALU.max if site == "kk" else ALU.add) if site in ROOTS else (hr_ready, ALU.add)
                first, rest = (7, 1) if site == "gqa" else (0, 1)
                ins = V.tensor_scalar(dst[:, 0:512], ps[0:8, first, :], scale, add, ALU.mult, op)
                if n > 512:
                    ins = V.tensor_scalar(dst[:, 512:n], ps[0:8, rest, 0:n - 512], scale, add, ALU.mult, op)
                ins.then_inc(sem_, 1)

            def head_factors(site, n):
                v.wait_ge(hrt_ready, ROOTS.index(site) + 1)
                m, y0, y = (t[:, 0:n] for t in factors_of(site))
                rsqrt(y, m, y0, y, None if site == "kk" else hr_ready)

            for c in range(8):
                ins = V.tensor_scalar(kk[:, c], pT2[:, K0 + c], col("k_k", c), None, ALU.mult)
            ins.then_inc(kk0_ready, 1)

            def by64(t):
                return t.rearrange("p c (k t) -> p (c k) t", t=64)

            v.wait_ge(mask2_in, 16)
            V.tensor_tensor(idc, ident[:, 0:HD], ident[:, HD:P], ALU.add).then_inc(idc_ready, 1)
            v.wait_ge(idc_ready, 1)

            def triangles(g):
                v.wait_ge(tp_ready, g + 1)
                V.tensor_tensor(Tp, ps[:, 7, :].rearrange("p (c t) -> p c t", t=HD), wmask[:, g // 4, 0:HD].unsqueeze(1).to_broadcast([P, 8, HD]), ALU.mult).then_inc(tp_done, 1)

            for d in range(2):
                v.wait_ge(zl_used, 16 * d + 8)
                for c in range(8):
                    ins = V.tensor_tensor_scan(LL[:, c], restart, lw[:, c], 0.0, ALU.mult, ALU.add)
                link(ins)
                link(V.tensor_copy(PC, LL.rearrange("p c (k t) -> p c k t", t=64)[:, :, :, 63]))
                if d == 1:
                    link(V.tensor_tensor(LL, lw, LL, ALU.subtract))
                    link(V.tensor_tensor(by64(LL), by64(LL), PC.rearrange("p c k -> p (c k)").unsqueeze(2).to_broadcast([P, 32, 64]), ALU.add))
                V.tensor_tensor(lw, LL, lw, ALU.subtract).then_inc(L_ready, 1)
                if d == 0:
                    head_sums("kk", 512, 1.0, 1e-30)
                    head_factors("kk", 512)
                    V.tensor_scalar(hK[2][:, 0:512], hK[2][:, 0:512], 1e12, None, ALU.min).then_inc(hr_ready, 1)
                A_, B_ = (b[:, :, :, 0].rearrange("p c k t -> p (c k) t") for b in (AQ, BG))
                GG = BG[:, :, :, 1].rearrange("p c k t -> p (c k) t")
                kd = ksum if d == 0 else pT2[:, K0:K0 + 8]
                v.wait_ge(zl_used, 16 * d + 16)
                for c in range(8):
                    ins = V.tensor_scalar(BG[:, c, :, 1], aa[:, c].rearrange("p (k t) -> p k t", t=64), -1.0, col("k_a", c), ALU.add, ALU.mult)
                link(ins)
                link(V.scalar_tensor_tensor(by64(kd), GG, 1.0, by64(pT2[:, K0:K0 + 8]), ALU.add, ALU.mult))
                if d == 0:
                    from_banks("kk", 4, lambda j, f: V.tensor_tensor(kk[:, 2 * j:2 * j + 2], kk[:, 2 * j:2 * j + 2], f, ALU.mult))
                v.wait_ge(e_ready, 3 * d + 1)
                V.tensor_tensor(A_, by64(kk), by64(EE), ALU.mult).then_inc(e_used, 1)
                link(V.tensor_tensor(aa, kk, aa, ALU.mult))
                v.wait_ge(e_ready, 3 * d + 3)
                V.tensor_tensor(GG, by64(kd), by64(lw), ALU.mult)
                V.tensor_tensor(B_, by64(aa), by64(lw), ALU.mult).then_inc(prep_done, 1)
                if d == 1:
                    V.tensor_tensor(ksum, ksum, kd, ALU.add)
                for g in range(4 * d, 4 * d + 4):
                    k = time_chunk(g)
                    mask = wmask[:, d].unsqueeze(1).to_broadcast([P, 4, P])
                    if g % 4 == 0:
                        triangles(g)
                    for q in range(4):
                        odd, half = q // 2, q % 2
                        if q == 2:
                            v.wait_ge(t_done, 12 * g + 2)
                            V.tensor_tensor(MT, ident.unsqueeze(1).to_broadcast([P, 8, P]), TR[:, 0], ALU.subtract).then_inc(nt0, 1)
                        v.wait_ge(ws_ready, 4 * g + q + 1)
                        V.tensor_tensor(WW[:, 4 * half:4 * half + 4, odd], ps[:, q, :].rearrange("p (c t) -> p c t", t=P), mask, ALU.mult).then_inc(w_done, 1)
                    for l in range(5):
                        for j in range(2):
                            v.wait_ge(x_ready, 10 * g + 2 * l + j + 1)
                            x = ps[:, j, 0:T].rearrange("p (c t) -> p c t", t=HD)
                            if l < 4:
                                V.tensor_tensor(Yc[:, 4 * j:4 * j + 4], idc.unsqueeze(1).to_broadcast([P, 4, HD]), x, ALU.subtract).then_inc(yt_done, 1)
                        for j in range(2):
                            for b in (0, HD):
                                x = ps[b:b + HD, j, 0:T].rearrange("p (c t) -> p c t", t=HD)
                                ins = V.tensor_tensor(YY[b:b + HD, 4 * j:4 * j + 4, b:b + HD], idc[b:b + HD].unsqueeze(1).to_broadcast([HD, 4, HD]), x, ALU.subtract)
                            ins.then_inc(yb_done, 1)
                    for j in range(2):
                        v.wait_ge(u_ready, 2 * g + j + 1)
                        V.tensor_copy(UV[0:64, 4 * j:4 * j + 4], ps[0:64, j, :].rearrange("p (c t) -> p c t", t=P)).then_inc(u_done, 1)
                    v.wait_ge(sp_done, g + 1)
                    for j in range(2):
                        v.wait_ge(dl_ready, 2 * g + j + 1)
                        V.tensor_tensor(PCM[:, 4 * j:4 * j + 4], ps[:, 2 + j, :].rearrange("p (c t) -> p c t", t=P), PCM[:, 4 * j:4 * j + 4], ALU.mult).then_inc(dl_used, 1)
                    v.wait_ge(ym_ready, g + 1)
                    out = ps[:, 4, :].rearrange("p (c t) -> p c t", t=64)
                    ys = YS[:, :, 64 * k:64 * k + 64]
                    if d == 0:
                        V.tensor_copy(ys, out).then_inc(yg_done, 1)
                    else:
                        V.tensor_tensor(ys, ys, out, ALU.add).then_inc(yg_done, 1)
                    if g % 4 < 3:
                        triangles(g + 1)
                    v.wait_ge(dl_used, 2 * g + 2)
                    V.tensor_tensor(BD, SP_, PCM, ALU.add).then_inc(bd_done, 1)
            v.wait_ge(yg_done, 8)
            head_sums("mean", 512, 1.0 / HD, 0.0)
            head_sums("gqa", 768, 1.0 / HD, EPS)
            from_banks("mean", 4, lambda j, f: V.tensor_tensor(YS[:, 2 * j:2 * j + 2], YS[:, 2 * j:2 * j + 2], f, ALU.subtract))
            head_factors("gqa", 768)
            for c in range(8):
                ins = V.scalar_tensor_tensor(rb[:, c], pT2[:, R0 + c], col("r_k", c), ksum[:, c], ALU.mult, ALU.mult)
            ins.then_inc(rb_ready, 1)
            from_banks("gqa", 5, lambda j, f: V.scalar_tensor_tensor(pT2[:, Q0 + 2 * j:Q0 + 2 * j + 2], pT2[:, Q0 + 2 * j:Q0 + 2 * j + 2],
                                                                     gq8 if j < 4 else col("k_norm2"), f, ALU.mult, ALU.mult))
            head_sums("var", 512, 1.0 / HD, GN_EPS)
            v.wait_ge(rope_in, 16)
            for j in range(5):
                qk = pT2[:, Q0 + 2 * j:Q0 + 2 * j + 2]
                v.wait_ge(bc_ready, banks_before("rope") + 5)
                link(V.tensor_tensor(rtmp, ps[:, 2 + j, :].rearrange("p (c t) -> p c t", t=T), sinT.unsqueeze(1).to_broadcast([P, 2, T]), ALU.mult))
                v.wait_ge(cos_done, 1)
                V.tensor_tensor(qk, qcos[:, 2 * j:2 * j + 2], rtmp, ALU.add).then_inc(bc_used, 1)
                v.wait_ge(bc_used, banks_before("rope") + j + 1)
                if j == 0:
                    head_factors("var", 512)
            from_banks("var", 4, lambda j, f: V.tensor_tensor(YS[:, 2 * j:2 * j + 2], YS[:, 2 * j:2 * j + 2], f, ALU.mult))
            head_sums("bonus", 512, 0.5, 0.0)
            for c in range(8):
                V.tensor_scalar(YS[:, c], YS[:, c], col("lnx_w", c), col("lnx_b", c), ALU.mult, ALU.add)
            from_banks("bonus", 4, lambda j, f: V.tensor_tensor(bv[:, 2 * j:2 * j + 2], pT2[:, V0 + 2 * j:V0 + 2 * j + 2], f, ALU.mult))
            link(V.tensor_tensor(YS, YS, bv, ALU.add))
            from_banks("gate", 4, lambda j, f: V.tensor_tensor(YS[:, 2 * j:2 * j + 2], YS[:, 2 * j:2 * j + 2], f, ALU.mult))

            def maxima(pc):
                for m in range(4 * pc, 4 * pc + 4):
                    q, odd = m // 2, m % 2
                    v.wait_ge(g_sc, m + 1)
                    V.reduce_max(g_negm[:, m:m + 1], ps[:, 4 + odd + 2 * (q % 2), 0:T], AX, negate=True).then_inc(g_max, 1)

            maxima(0)
            maxima(1)
            for pc in range(8):
                v.wait_ge(g_exp, 4 * pc + 4)
                link(V.reciprocal(g_den[:, 4 * pc:4 * pc + 4], g_den[:, 4 * pc:4 * pc + 4]))
                for m in range(4 * pc, 4 * pc + 4):
                    ins = V.tensor_scalar(PR2[:, m], PR2[:, m], g_den[:, m:m + 1], None, ALU.mult)
                ins.then_inc(g_psc, 1)
                if pc < 6:
                    maxima(pc + 2)
                if pc >= 1:
                    v.wait_ge(g_pv, 2 * pc)
                    V.tensor_copy(yA[:, pc - 1], ps[:, 2 + (pc - 1) % 2, 0:T]).then_inc(y_ready, 1)
            v.wait_ge(g_pv, 16)
            V.tensor_copy(yA[:, 7], ps[:, 3, 0:T]).then_inc(y_ready, 1)
            v.wait_ge(y_ready, 16)
            split_lo(1, [YS[:, 0:4], YS[:, 4:8], yA[:, 0:4], yA[:, 4:8]])
            for_units(v, "w_out2", lo_part(v, V, "w_out2"), add_to_x("w_out2"))
            ahead("w_pq")
            v.wait_ge(freed, stage_done("w_out2"))
            norm(3, "norm2")
            for_units(v, "w_pq", lo_part(v, V, "w_pq"), lambda u, r: None)
            v.wait_ge(ks_copied, 8)
            lists = [(u, hp) for u in range(2) for hp in range(16)]
            for u, hp in lists:
                ins = V.max(topv[:, u, hp, 0:8], s1[:, u, hp])
            link(ins)
            for u, hp in lists:
                V.max_index(topi[:, u, hp, 0:8], topv[:, u, hp, 0:8], s1[:, u, hp])
                ins = V.match_replace(s2[:, u, hp], topv[:, u, hp, 0:8], s1[:, u, hp], LOWEST)
            link(ins)
            for u, hp in lists:
                ins = V.max(topv[:, u, hp, 8:16], s2[:, u, hp])
            link(ins)
            for u, hp in lists:
                ins = V.max_index(topi[:, u, hp, 8:16], topv[:, u, hp, 8:16], s2[:, u, hp])
            link(ins)
            V.tensor_copy(topif, topi)
            for u in range(2):
                a, b = topv[:, u, 0::2], topv[:, u, 1::2]
                ins = V.tensor_tensor(cand[:, u], a.unsqueeze(3).to_broadcast([P, 8, 16, 16]), b.unsqueeze(2).to_broadcast([P, 8, 16, 16]), ALU.add)
            link(ins)
            lists = [(u, h) for u in range(2) for h in range(8)]
            flat = cand.rearrange("p u h a b -> p u h (a b)")
            for u, h in lists:
                ins = V.max(best[:, u, h, 0:8], flat[:, u, h])
            link(ins)
            for u, h in lists:
                V.max_index(bi[:, u, h, 0:8], best[:, u, h, 0:8], flat[:, u, h])
                ins = V.match_replace(cand2[:, u, h], best[:, u, h, 0:8], flat[:, u, h], LOWEST)
            link(ins)
            for u, h in lists:
                ins = V.max(best[:, u, h, 8:16], cand2[:, u, h])
            link(ins)
            for u, h in lists:
                ins = V.max_index(bi[:, u, h, 8:16], best[:, u, h, 8:16], cand2[:, u, h])
            link(ins)
            gate = e12g[:, 2].rearrange("p u (h n) -> p u h n", h=8)
            V.tensor_tensor(gate, best, best[:, :, :, 0:1].to_broadcast([P, 2, 8, 16]), ALU.subtract).then_inc(gd_ready, 1)
            bflat = bi.rearrange("p u h n -> p (u h n)")
            V.tensor_single_scalar(ab[:, 0:256], bflat, 4, ALU.logical_shift_right)
            link(V.tensor_single_scalar(ab[:, 256:512], bflat, 15, ALU.bitwise_and))
            link(V.tensor_copy(abf.rearrange("p v u h n -> p (v u h n)"), ab))
            iota16 = iota[:, 0:16].unsqueeze(1).unsqueeze(1).to_broadcast([P, 8, 16, 16])
            for e in range(2):
                for u in range(2):
                    link(V.tensor_tensor(big1, abf[:, e, u].unsqueeze(3).to_broadcast([P, 8, 16, 16]), iota16, ALU.is_equal))
                    link(V.tensor_tensor(big2, big1, topif[:, u, e::2].unsqueeze(2).to_broadcast([P, 8, 16, 16]), ALU.mult))
                    link(V.reduce_sum(e12g[:, e, u].rearrange("p (h n) -> p h n", h=8), big2, AX))
            v.wait_ge(ge_ready, 1)
            link(V.reduce_sum(gsum, gate, AX))
            link(V.reciprocal(gsum, gsum))
            V.tensor_tensor(gate, gate, gsum.unsqueeze(3).to_broadcast([P, 2, 8, 16]), ALU.mult).then_inc(slots_ready, 1)
            v.wait_ge(et_done, 2)

            def gate_raw(i, r):
                v.wait_ge(g_out, 8 * i + (r + 1))
                raw = G3[:, P - RAW:P, bass.ds(16 * i + 2 * r, 2)]
                V.tensor_tensor(raw, raw, ps[:, 2 + r % 4, 0:T].rearrange("p (t e) -> p e t", t=2)[:, P - RAW:P], ALU.mult).then_inc(raw_gated, 1)

            def onehots(i, waits):
                for r in range(8):
                    if waits or r >= 4:
                        v.wait_ge(g_mm, 8 * i + (r - 3))
                    V.tensor_tensor(OH[:, r % 4], iota.unsqueeze(1).unsqueeze(1).to_broadcast([P, 2, 2, P]),
                                    ET[:, 0:2, bass.ds(16 * i + 2 * r, 2)].unsqueeze(3).to_broadcast([P, 2, 2, P]), ALU.is_equal).then_inc(oh_ready, 1)
                    if r >= 3:
                        gate_raw(i, r - 3)
                    elif waits:
                        gate_raw(i - 1, r + 5)
            onehots(0, False)
            with v.Fori(1, T // 16) as i:
                onehots(i, True)
            for r in range(5, 8):
                gate_raw(T // 16 - 1, r)
            v.wait_ge(g_out, T // 2)
            v.wait_ge(raw_gated, T // 2)

            def gated(u, r):
                v.wait_ge(freed, u + (UNIT0["u_tab"] + 1))
                V.tensor_tensor(gm[:, r], gl[:, r], G3[:, u - RAW], ALU.mult).then_inc(gm_done, 1)
                v.wait_ge(gm_done, u + (1 - RAW))
                V.tensor_copy(Gb[:, u - RAW, 0], gm[:, r]).then_inc(hidhi_done, 1)
                v.wait_ge(hidhi_done, u + (65 - RAW))
                V.tensor_tensor(Gb[:, u - RAW, 1], gm[:, r], Gb[:, u - RAW, 0], ALU.subtract).then_inc(hid_done, 1)

            def gated_and_split(u, r):
                gated(u, r)
                V.tensor_copy(gr[:, r], G3[:, u + (P - 2 * RAW)]).then_inc(raw_out, 1)
                v.wait_ge(raw_out, u + (1 - RAW))
                V.tensor_copy(Gb[:, u + (P - 2 * RAW), 0], gr[:, r]).then_inc(raw_hi, 1)
                v.wait_ge(raw_hi, u + (1 - RAW))
                V.tensor_tensor(Gb[:, u + (P - 2 * RAW), 1], gr[:, r], Gb[:, u + (P - 2 * RAW), 0], ALU.subtract).then_inc(raw_done, 1)
            for_units(v, "u_tab", lo_part(v, V, "u_tab"), gated_and_split, RAW, 2 * RAW)
            for_units(v, "u_tab", lo_part(v, V, "u_tab"), gated, 2 * RAW)
            ahead("v_tab")
            for_units(v, "v_tab", lo_part(v, V, "v_tab"), add_to_x("v_tab"))
            v.wait_ge(freed, stage_done("v_tab"))
            norm(4, "normf")

        @block.tensor
        def _(pe):
            mm, tr = PE.matmul, PE.transpose

            def norm(n):
                if n:
                    pe.wait_ge(acc_done, KD * n)
                    ins = mm(ps[:, 7, 0:T], ones, n_acc, start=True, stop=True)
                else:
                    pe.wait_ge(sq_added, 5)
                    ins = mm(ps[:, 7, 0:T], ones, scr[:, 0], start=True, stop=True)
                ins.then_inc(ms_ready, 1)

            def product(name, hi, lo, first=0, stop=None, parts_ready=None):
                n, per, b0, u0 = UNITS[name], PER[name], BLOCK0[name], UNIT0[name]

                def pair(i, by_group):
                    for r in range(2):
                        pe.wait_ge(freed, 2 * i + (u0 + r - 1))
                        for j in range(per):
                            slot = (per * r + j) % RING
                            pe.wait_ge(lo_done, 2 * per * i + (b0 + per * r + j + 1))
                            for k in range(HALF):
                                kt = j * HALF + k
                                first, last = kt == 0, kt == per * HALF - 1
                                if by_group and r == 0 and kt % 4 == 0:
                                    pe.wait_ge(parts_ready[0], parts_ready[1] + kt // 4 + 1)
                                mm(ps[:, r, 0:T], sv[:, slot, 0, k], hi(kt), start=first, stop=False)
                                mm(ps[:, r, 0:T], sv[:, slot, 0, k], lo(kt), start=False, stop=False)
                                ins = mm(ps[:, r, 0:T], sv[:, slot, 1, k], hi(kt), start=False, stop=last)
                            ins.then_inc(blk_mm, 1)
                if parts_ready:
                    pair(0, True)
                with pe.Fori(1 if parts_ready else first // 2, (stop or n) // 2) as i:
                    pair(i, False)

            def from_h(name, first=0, stop=None, parts_ready=None):
                product(name, lambda kt: h_hi[:, kt], lambda kt: h_lo[:, kt], first, stop, parts_ready)

            pe.wait_ge(const_in, 32)
            norm(0)

            def w_in_pair(i, waits):
                for r in range(2):
                    if waits:
                        pe.wait_ge(freed, 2 * i + (r - 1))
                    for j in range(2):
                        pe.wait_ge(w_arrived[2 * r + j], 16 * i + 16)
                        for k in range(HALF):
                            kt = HALF * j + k
                            if not waits and r == 0 and kt % 4 == 0:
                                pe.wait_ge(hf_ready, kt // 4 + 1)
                            ins = mm(ps[:, r, 0:T], wv[:, 2 * r + j, k], scr[:, kt], start=kt == 0, stop=kt == KD - 1)
                        ins.then_inc(f_mm, 1)
            w_in_pair(0, False)
            with pe.Fori(1, UNITS["w_in"] // 2) as i:
                w_in_pair(i, True)
            pe.wait_ge(freed, 44)
            for tt in range(2):
                for c in range(4):
                    ins = tr(ps[:, 2 + tt, c * P:(c + 1) * P], pT[:, 4 + c, tt * P:(tt + 1) * P], ident)
                ins.then_inc(tr_ready, 1)
            for tt in range(2):
                for c in range(6):
                    ins = tr(ps[:, 4 + 2 * tt + c // 4, (c % 4) * P:(c % 4 + 1) * P], pT[:, 38 + c, tt * P:(tt + 1) * P], ident)
                ins.then_inc(tr_ready, 1)
            pe.wait_ge(mask_in, 48)
            pe.wait_ge(sq_heads, 1)
            for c in range(12):
                g = c // 4
                ins = mm(ps[0:8, g // 2, (g % 2) * T:(g % 2 + 1) * T], sel8[:, c % 4], qk_sq[:, c], start=c % 4 == 0, stop=c % 4 == 3)
            ins.then_inc(hs_ready, 1)
            pe.wait_ge(sguw_ready, 1)
            for n in range(2):
                pe.wait_ge(tr_freed, n + 1 if n == 0 else 2)
                if n == 0:
                    pe.wait_ge(tr_freed, 2)
                for h in range(8):
                    b = HD * (h % 2)
                    ins = mm(ps[b:b + HD, 2 + n, (h // 2) * P:(h // 2 + 1) * P], vtok_a[:, n, h * HD:(h + 1) * HD], sguw[:, h], start=True, stop=True)
                ins.then_inc(mix_ready, 1)
            pe.wait_ge(tr_freed, 6)
            pe.wait_ge(hr_ready, 1)
            for c in range(12):
                ins = mm(ps[:, (4 + c // 2) % 8, (c % 2) * T:(c % 2 + 1) * T], selT8[:, c % 4], hsy[:, (c // 4) * T:(c // 4 + 1) * T], start=True, stop=True)
                if c % 2:
                    ins.then_inc(bc_ready, 1)
            pe.wait_ge(y_ready, 2)
            pe.wait_ge(bc_used, 6)
            for m in range(24):
                q, odd = m // 2, m % 2
                hd, qt = 2 * (q // 2) + odd, q % 2
                b, w = HD * odd, P * (qt + 1)
                if m >= 6:
                    pe.wait_ge(sc_used, m - 5)
                mm(ps[:, 2 + odd + 2 * (q % 3), 0:w], pT[b:b + HD, 26 + hd // 2, qt * P:(qt + 1) * P],
                   pT[b:b + HD, 32 + hd // 2, 0:w], start=True, stop=True).then_inc(sc_ready, 1)

            def pt(hd):
                pe.wait_ge(psc_ready, hd + 1)
                if hd >= 2:
                    pe.wait_ge(pt_copied, hd - 1)
                tr(ps[:, 2 + hd % 2, 0:P], PR[:, 2 * hd, 0:P], ident)
                tr(ps[:, 2 + hd % 2, P:2 * P], PR[:, 2 * hd + 1, 0:P], ident)
                tr(ps[:, 2 + hd % 2, 2 * P:3 * P], PR[:, 2 * hd + 1, P:2 * P], ident).then_inc(pt_ready, 1)

            pt(0)
            for hd in range(12):
                if hd < 11:
                    pt(hd + 1)
                pe.wait_ge(pt_copied, hd + 1)
                if hd >= 4 and hd % 2 == 0:
                    pe.wait_ge(y_ready, 2 + hd // 2 - 1)
                b, o = HD * (hd % 2), 4 + (hd // 2) % 2
                mm(ps[b:b + HD, o, 0:T], vtok_c[:, 0, hd * HD:(hd + 1) * HD], PTs[:, hd % 2, 0:T], start=True, stop=False)
                mm(ps[b:b + HD, o, P:T], vtok_c[:, 1, hd * HD:(hd + 1) * HD], PTs[:, hd % 2, T:T + P], start=False, stop=True).then_inc(pv_ready, 1)
            from_h("w_out", parts_ready=(y_split, 0))
            norm(1)
            from_h("mlp_in", parts_ready=(h_ready, 0))
            pe.wait_ge(hid_done, 64)
            product("mlp_out", lambda kt: hid[:, 0, kt], lambda kt: hid[:, 1, kt])
            norm(2)
            from_h("w_in2", parts_ready=(h_ready, 4))
            pe.wait_ge(freed, stage_done("w_in2"))

            def head_sums(site, src, n):
                if site != "gqa":
                    pe.wait_ge(hr_ready, SUMS.index(site))
                for c in range(n):
                    g = c // 4
                    bank = (7 if g < 2 else 1) if site == "gqa" else 0
                    ins = mm(ps[0:8, bank, (g % 2) * T:(g % 2 + 1) * T], sel8[:, c % 4], src[:, c], start=c % 4 == 0, stop=c % 4 == 3 or c == n - 1)
                ins.then_inc(hs_ready, 1)

            def to_channels(site, n, fn):
                pe.wait_ge(bc_used, banks_before(site))
                for c in range(n):
                    ins = fn(ps[:, 2 + c // 2, (c % 2) * T:(c % 2 + 1) * T], c)
                    if c % 2:
                        ins.then_inc(bc_ready, 1)

            def heads_back(site, n):
                pe.wait_ge(hr_ready, SUMS.index(site) + 1)
                y = factors_of(site)[2]
                to_channels(site, n, lambda out, c: mm(out, selT8[:, c % 4], y[:, (c // 4) * T:(c // 4 + 1) * T], start=True, stop=True))

            for d in range(2):
                pe.wait_ge(lora_in, 16 * d + 16)
                pe.wait_ge(lin_ready, 2)
                if d == 1:
                    pe.wait_ge(bd_done, 4)
                    pe.wait_ge(yg_done, 4)
                for w in range(2):
                    for c in range(8):
                        ins = mm(ps[:, 4 * w + c // 2, (c % 2) * T:(c % 2 + 1) * T], lora[:, w * 1024 + c * P:w * 1024 + (c + 1) * P],
                                 pT2[:, (AL if w else WL) + d], start=True, stop=True)
                        if c % 2:
                            ins.then_inc(zl_ready, 1)
                if d == 0:
                    pe.wait_ge(sq_heads, 2)
                    pe.wait_ge(zl_used, 2)
                    head_sums("kk", kk_sq, 8)
                    pe.wait_ge(zl_used, 12)
                    heads_back("kk", 8)
                    pe.wait_ge(zl_used, 16)
                pe.wait_ge(prep_done, d + 1)
                pe.wait_ge(q_done, d + 1)
                for g in range(4 * d, 4 * d + 4):
                    k = time_chunk(g)
                    for c in range(8):
                        for b in (0, HD):
                            ins = mm(ps[b:b + HD, 7, c * HD:(c + 1) * HD], BG[b:b + HD, c, k, 0], AQ[b:b + HD, c, k, 0], start=True, stop=True)
                    ins.then_inc(tp_ready, 1)

                    def v_to_tokens(j):
                        for c in range(4):
                            ins = tr(ps[:, 6 + j, c * P:(c + 1) * P], words((V0 + 4 * j + c) * T + 64 * k - 64, P), ident)
                        ins.then_inc(vt_ready, 1)

                    v_to_tokens(0)
                    for j in (1, 0):
                        if j == 0 and g % 4:
                            pe.wait_ge(yg_done, g)
                        for c in range(4):
                            ins = tr(ps[:, 4 + j, c * P:(c + 1) * P], BG[:, 4 * j + c, k].rearrange("p v t -> p (v t)"), ident)
                        ins.then_inc(bt_ready, 1)
                    pe.wait_ge(tp_done, g + 1)
                    v_to_tokens(1)
                    for q in range(4):
                        odd, half = q // 2, q % 2
                        b = HD * odd
                        if q == 2:
                            pe.wait_ge(dl_used, 2 * g)
                        for c in range(4 * half, 4 * half + 4):
                            ins = mm(ps[:, q, (c % 4) * P:(c % 4 + 1) * P], BG[b:b + HD, c, k].rearrange("p v t -> p (v t)"),
                                     AQ[b:b + HD, c, k].rearrange("p v t -> p (v t)"), start=True, stop=True)
                        ins.then_inc(ws_ready, 1)
                    pe.wait_ge(nt0, g + 1)
                    pe.wait_ge(w_done, 4 * g + 2)
                    for c in range(8):
                        ins = mm(ps[:, c // 4, (c % 4) * HD:(c % 4 + 1) * HD], MT[:, c], idc, start=True, stop=True)
                        if c % 4 == 3:
                            ins.then_inc(n0_ready, 1)
                    for l in range(5):
                        pe.wait_ge(t_done, 12 * g + 2 * l + 4)
                        for c in range(8):
                            if c % 4 == 0:
                                if l == 0:
                                    pe.wait_ge(n0_done, 2 * g + c // 4 + 1)
                                else:
                                    pe.wait_ge(mc_done, 8 * g + 2 * (l - 1) + c // 4 + 1)
                            ins = mm(ps[:, c // 4, (c % 4) * HD:(c % 4 + 1) * HD], TR[:, (l + 1) % 2, c], Mc[:, c], start=True, stop=True)
                            if c % 4 == 3:
                                ins.then_inc(x_ready, 1)
                        for c in range(8):
                            if c % 4 == 0 and l:
                                pe.wait_ge(mt_done, 10 * g + 2 * (l - 1) + c // 4 + 1)
                            if l < 4:
                                if c % 4 == 0:
                                    pe.wait_ge(yt_done, 8 * g + 2 * l + c // 4 + 1)
                                    pe.wait_ge(w_done, 4 * g + 4)
                                ins = mm(ps[:, 2 + c // 4, (c % 4) * HD:(c % 4 + 1) * HD], MT[:, c], Yc[:, c], start=True, stop=True)
                                if c % 4 == 3:
                                    ins.then_inc(m_mm, 1)
                        for c in range(8):
                            if c % 4 == 0:
                                pe.wait_ge(yb_done, 10 * g + 2 * l + c // 4 + 1)
                                if l == 0:
                                    pe.wait_ge(bt_copied, 2 * g + 2)
                            ins = mm(ps[:, 4 + c // 4, (c % 4) * P:(c % 4 + 1) * P], YY[:, c], MT[:, c], start=True, stop=True)
                            if c % 4 == 3:
                                ins.then_inc(mt_mm, 1)
                    pe.wait_ge(vt_copied, 2 * g + 2)
                    if g % 4 == 0:
                        pe.wait_ge(bd0, d + 1)
                    else:
                        pe.wait_ge(bd_done, g)
                    for c in range(8):
                        for odd in range(2):
                            b = HD * odd
                            o = ps[b:b + HD, 6 + c // 4, (c % 4) * HD:(c % 4 + 1) * HD]
                            mm(o, AQ[:, c, k, 0], BD[:, c, b:b + HD], start=True, stop=False)
                            ins = mm(o, WW[64:128, c, odd, 0:64], UV[64:128, c, b:b + HD], start=False, stop=True)
                        if c % 4 == 3:
                            ins.then_inc(r_ready, 1)
                    for c in range(8):
                        if c % 4 == 0:
                            pe.wait_ge(rs_done, 2 * g + c // 4 + 1)
                            pe.wait_ge(mt_done, 10 * g + 8 + c // 4 + 1)
                        for odd in range(2):
                            ins = mm(ps[0:64, c // 4, (c % 4) * P + HD * odd:(c % 4) * P + HD * odd + HD], MT[:, c, HD * odd:HD * odd + HD], RS[:, c], start=True, stop=True)
                        if c % 4 == 3:
                            ins.then_inc(u_ready, 1)
                    for c in range(8):
                        if c % 4 == 0:
                            pe.wait_ge(u_done, 2 * g + c // 4 + 1)
                        ins = mm(ps[:, 2 + c // 4, (c % 4) * P:(c % 4 + 1) * P], BGt[:, c], UV[:, c], start=True, stop=True)
                        if c % 4 == 3:
                            ins.then_inc(dl_ready, 1)
                    for c in range(8):
                        for odd in range(2):
                            mm(ps[HD * odd:HD * odd + HD, 4, c * 64:c * 64 + 64], BD[:, c, HD * odd:HD * odd + HD], AQ[:, c, k, 1], start=True, stop=False)
                            ins = mm(ps[HD * odd:HD * odd + HD, 4, c * 64:c * 64 + 64], UV[:, c, HD * odd:HD * odd + HD], WW[:, c, odd, 64:128], start=False, stop=True)
                    ins.then_inc(ym_ready, 1)
            pe.wait_ge(yg_done, 8)
            pe.wait_ge(bd_done, 8)
            head_sums("mean", YS, 8)
            pe.wait_ge(sq_heads, 3)
            head_sums("gqa", sq2, 10)
            heads_back("mean", 8)
            heads_back("gqa", 10)
            pe.wait_ge(sq_heads, 4)
            head_sums("var", sq2, 8)
            pe.wait_ge(rope_in, 16)
            pe.wait_ge(bc_used, banks_before("rope"))
            to_channels("rope", 10, lambda out, c: mm(out, perm, pT2[:, Q0 + c], start=True, stop=True))
            heads_back("var", 8)
            pe.wait_ge(rb_ready, 1)
            head_sums("bonus", rb, 8)
            heads_back("bonus", 8)
            pe.wait_ge(lora_in, 48)

            def gate_sums(out, c):
                mm(out, lora[:, c * P:(c + 1) * P], pT2[:, GL], start=True, stop=False)
                return mm(out, lora[:, 1024 + c * P:1024 + (c + 1) * P], pT2[:, GL + 1], start=False, stop=True)
            to_channels("gate", 8, gate_sums)
            for tt in range(2):
                for c in range(2):
                    ins = tr(ps[:, 7, (2 * tt + c) * P:(2 * tt + c + 1) * P], pT2[:, VV0 + c, tt * P:(tt + 1) * P], ident)
            ins.then_inc(v2_ready, 1)
            pe.wait_ge(bc_used, banks_before("gate") + 4)
            pe.wait_ge(v2_copied, 1)

            def scores(pc):
                for m in range(4 * pc, 4 * pc + 4):
                    q, odd = m // 2, m % 2
                    b, qt = HD * odd, q % 2
                    if m >= 4:
                        pe.wait_ge(g_exp, m - 3)
                    mm(ps[:, 4 + odd + 2 * (q % 2), 0:T], pT2[b:b + HD, Q0 + pc, qt * P:(qt + 1) * P], pT2[b:b + HD, KK0 + pc // 4], start=True, stop=True).then_inc(g_sc, 1)

            scores(0)
            scores(1)
            for pc in range(8):
                pe.wait_ge(g_psc, pc + 1)
                for odd in range(2):
                    if pc:
                        pe.wait_ge(g_ptc, 2 * (pc - 1) + odd + 1)
                    for kt in range(2):
                        for qt in range(2):
                            ins = tr(ps[:, odd, kt * T + qt * P:kt * T + (qt + 1) * P], PR2[:, 4 * pc + 2 * qt + odd, kt * P:(kt + 1) * P], ident)
                    ins.then_inc(g_pt, 1)
                if pc < 6:
                    scores(pc + 2)
                for odd in range(2):
                    pe.wait_ge(g_ptc, 2 * pc + odd + 1)
                    if pc >= 2:
                        pe.wait_ge(y_ready, 8 + pc - 1)
                    kv = 2 * (pc // 4) + odd
                    for kt in range(2):
                        ins = mm(ps[HD * odd:HD * odd + HD, 2 + pc % 2, 0:T], vtok2[:, kt, kv * HD:(kv + 1) * HD], PT2[:, odd, kt * T:(kt + 1) * T], start=kt == 0, stop=kt == 1)
                    ins.then_inc(g_pv, 1)
            from_h("w_out2", parts_ready=(y_split, 4))
            norm(3)
            from_h("w_pq", parts_ready=(h_ready, 8))
            pe.wait_ge(freed, stage_done("w_pq"))
            pe.wait_ge(sk_in, 16)
            for j in range(8):
                for hp in range(4 * (j % 4), 4 * (j % 4) + 4):
                    ins = mm(ps[:, (2 + j) % 8, (hp % 4) * P:(hp % 4 + 1) * P], qT2[:, hp, (j // 4) * P:(j // 4 + 1) * P], skT[:, hp], start=True, stop=True)
                ins.then_inc(ks_ready, 1)
            pe.wait_ge(ks_copied, 8)
            from_h("u_tab", 0, RAW)
            pe.wait_ge(slots_ready, 1)
            for n in range(3):
                for u in range(2):
                    ins = tr(ps[:, 2 + n // 2, (n % 2) * T + u * P:(n % 2) * T + (u + 1) * P], e12g[:, n, u], ident)
            ins.then_inc(slotsT, 1)
            pe.wait_ge(et_done, 2)

            def gates(i, waits):
                for r in range(8):
                    pe.wait_ge(ohg_ready, 8 * i + (r + 1))
                    if waits or r >= 4:
                        pe.wait_ge(raw_gated, 8 * i + (r - 3))
                    for t in range(2):
                        ins = mm(ps[:, 2 + r % 4, t * P:(t + 1) * P], OH[:, r % 4, 0, t], OH[:, r % 4, 1, t], start=True, stop=True)
                    ins.then_inc(g_mm, 1)
            gates(0, False)
            with pe.Fori(1, T // 16) as i:
                gates(i, True)
            from_h("u_tab", RAW)
            pe.wait_ge(hid_done, 64 + P - RAW)
            pe.wait_ge(raw_done, RAW)
            product("v_tab", lambda kt: Gb[:, kt, 0], lambda kt: Gb[:, kt, 1])
            norm(4)

    return nc


def blocks(w):
    k, n = w.shape
    return np.ascontiguousarray(w.reshape(k // (HALF * P), HALF, P, n // P, P).transpose(3, 0, 2, 1, 4)).reshape(-1, P, BLK)


def chunked(v):
    return np.ascontiguousarray(np.asarray(v).reshape(-1, P).T)


def constants():
    f = np.float32
    p, n = np.arange(P)[:, None], np.arange(P)[None]
    main = np.concatenate([(p == n), np.ones((P, P)), (p // HD == n // HD), np.broadcast_to(n, (P, P))], axis=1).astype(f)
    sel = np.zeros((P, 544), f)
    for c in range(4):
        for ch in range(P):
            sel[ch, 8 * c + 2 * c + ch // HD] = 1
            sel[2 * c + ch // HD, 32 + P * c + ch] = 1
    dm = np.zeros((P, 3, 2, T), f)
    for g, (window, d) in enumerate(((128, 1), (512, 4), (2048, 16))):
        for qt in range(2):
            q, k = qt * P + np.arange(P)[:, None], np.arange(T)[None]
            ok = (k <= q) & ((q - k) % d == 0) & (q - k <= window)
            dm[:, g, qt] = np.where(ok, 0, NEG)
    s, t = np.arange(64)[:, None], np.arange(64)[None]
    rw = np.zeros((P, 896), f)
    for d, (a, q) in enumerate((((s < t), (s <= t)), ((s > t), (s >= t)))):
        rw[:, d * P:(d + 1) * P] = np.tile(np.concatenate([a, q], axis=1), (2, 1))
    for l in range(6):
        rw[:, 256 + 64 * l:320 + 64 * l] = np.tile((s >> (l + 1) == t >> (l + 1)) & (s >> l != t >> l), (2, 1))
    rw[:, 640:] = np.arange(T)[None] % 64 != 0
    ch, tok = np.arange(P) % HD, np.arange(T)
    inv = f(10000.0) ** (-np.arange(0, 32, 2, dtype=f) / f(32))
    pos = np.where((ch < 32)[:, None], (tok // 64)[None], (tok % 64)[None]).astype(f)
    ang = pos * inv[ch % 16][:, None]
    turn = np.zeros((P, P), f)
    for m in range(P):
        if m % 32 < 16:
            turn[m + 16, m] = -1
        else:
            turn[m - 16, m] = 1
    rope = np.concatenate([np.cos(ang), np.sin(ang), turn], axis=1).astype(f)
    return {"cst_main": main, "cst_sel": sel, "dmask": dm.reshape(P, -1), "cst_rw": rw, "cst_rope": rope}


def layout(i):
    g = {k: np.asarray(v) for k, v in i.items()}
    a = dict(constants())
    a["x"] = np.ascontiguousarray(g["x"][0].T.reshape(KD, P, T).transpose(1, 0, 2)).reshape(P, KD * T)
    a["w_in"] = blocks(g["w_in"][0])
    a["w_out"] = blocks(g["w_out"][0])
    a["mlp_in"] = blocks(g["w_mlp_in"][0])
    a["mlp_out"] = blocks(g["w_mlp_out"][0])
    a["sgu_w"] = np.ascontiguousarray(g["sgu_w"][0].transpose(2, 0, 1)).reshape(P, -1)
    a["sgu_b"] = np.ascontiguousarray(np.repeat(g["sgu_b"][0], HD, axis=0).reshape(4, P, P).transpose(1, 0, 2)).reshape(P, -1)
    src = {"attn_norm": g["attn_norm"][0], "mlp_norm": g["mlp_norm"][0], "norm1": g["norm1_w_2"][0], "norm2": g["norm2_w_2"][0],
           "normf": g["normf_w_2"], "conv_w": g["conv_w"][0].reshape(-1), "q_norm": np.tile(g["q_norm"][0], 2),
           "k_norm": np.tile(g["k_norm"][0], 2), "q_norm2": np.tile(g["q_norm_w_2"][0], 2), "k_norm2": np.tile(g["k_norm_w_2"][0], 2),
           "mu_prev": spread(g["mu_prev_2"][0][None])[0], "mu_next": spread(g["mu_next_2"][0][None])[0],
           "w0": g["w0_2"][0].reshape(-1), "a0": g["a0_2"][0].reshape(-1), "k_k": g["k_k_2"][0], "k_a": g["k_a_2"][0],
           "r_k": g["r_k_2"][0].reshape(-1), "lnx_w": g["lnx_w_2"][0], "lnx_b": g["lnx_b_2"][0]}
    a["params"] = np.ascontiguousarray(np.concatenate([chunked(src[n]) for n, _ in PARAMS], axis=1))
    a["w_in2"] = blocks(spread(g["w_in_2"][0]))
    w = g["w_out_2"][0]
    a["w_out2"] = blocks(np.concatenate([w[:1024], w[1024:].reshape(16, HD, D)[Q_ORDER].reshape(1024, D)]))
    a["w_pq"] = blocks(g["w_pq_2"][0])
    a["u_tab"] = np.ascontiguousarray(g["u_tab_2"][0].reshape(P, P, 2, HALF, P).transpose(1, 2, 4, 3, 0)[np.roll(np.arange(P), RAW)]).reshape(-1, P, BLK)
    a["v_tab"] = np.ascontiguousarray(g["v_tab_2"][0].reshape(P, 16, HALF, KD, P).transpose(3, 1, 0, 2, 4)).reshape(-1, P, BLK)
    lora = np.zeros((2, P, 2, 1024), np.float32)
    lora[:, :96, 0] = g["w2_2"][0]
    lora[:, :96, 1] = g["a2_2"][0]
    a["lora"] = lora.reshape(2, P, -1)
    a["gate_w"] = np.ascontiguousarray(g["g2_2"][0].reshape(2, P, 1024).transpose(1, 0, 2)).reshape(P, -1)
    a["subkeys"] = np.ascontiguousarray(g["sub_keys_2"][0].reshape(16, P, P).transpose(2, 0, 1)).reshape(P, -1)
    return a


Q_ORDER = [0, 4, 1, 5, 2, 6, 3, 7, 8, 12, 9, 13, 10, 14, 11, 15]


def spread(w):
    out = np.zeros((w.shape[0], 42 * P), w.dtype)
    out[:, 0:3072] = w[:, 0:3072]
    for j in range(4):
        out[:, 3072 + P * j:3072 + P * j + 96] = w[:, 3072 + 96 * j:3168 + 96 * j]
    out[:, 3584:3840] = w[:, 3456:3712]
    if w.shape[1] > 3712:
        q = w[:, 3712:4736].reshape(-1, 16, HD)[:, Q_ORDER].reshape(-1, 1024)
        out[:, 3840:4864] = q
        out[:, 4864:5376] = w[:, 4736:5248]
    return out


_INS = ["cst_main", "cst_sel", "dmask", "cst_rw", "cst_rope", "params", "x", "sgu_w", "sgu_b", "lora", "gate_w", "subkeys",
        "w_in", "w_out", "mlp_in", "mlp_out", "w_in2", "w_out2", "w_pq", "u_tab", "v_tab"]


def kernel(**inputs):
    import concourse.bacc as bacc
    from concourse.bass_utils import run_bass_kernel_spmd

    nc = bacc.Bacc("TRN2", target_bir_lowering=False, num_devices=1)
    arrays = layout(inputs)
    A = {n: nc.dram_tensor("in_" + n, arrays[n].shape, F32, kind="ExternalInput").ap() for n in _INS}
    A["out"] = nc.dram_tensor("out", (P, KD * T), F32, kind="ExternalOutput").ap()
    build(nc, A)
    r = run_bass_kernel_spmd(nc, [{"in_" + n: arrays[n] for n in _INS}], core_ids=[0])
    out = r.results[0]["out"]
    return np.ascontiguousarray(out.reshape(P, KD, T).transpose(2, 1, 0)).reshape(1, T, D)
```
